# Optimizing a Trainium2 kernel written in Bass

```python
import jax, jax.numpy as jnp
from jax import lax
import numpy as np

D_MODEL = 1024
BATCH = 1
SEQ = 256
DEPTH = 1

CHUNK = 64
MIX_W = D_MODEL
POOL_W = MIX_W // 2
CONV_W = MIX_W - POOL_W
POOL_WINDOWS = (2, 4, 8, 16)
N_POOL_GROUPS = len(POOL_WINDOWS)
POOL_GROUP_W = POOL_W // N_POOL_GROUPS
N_CONV_GROUPS = 4
CONV_K = 3
IN_PROJ_W = POOL_W + 3 * CONV_W
MEM_LEN = 256
N_XHEADS = 4
XHEAD_DIM = D_MODEL // N_XHEADS
N_EXPERTS = 32
TOP_K = 4
D_FF = D_MODEL
SWIGLU_LIMIT = 7.0
SWIGLU_ALPHA = 1.702
EXPERT_BLOCK = 256
RMS_EPS = 1e-5

kernel_name = "hybrid_pool_conv_xattn_moe_encoder"

def rmsnorm(x, g):
    xf = x.astype(jnp.float32)
    y = xf * lax.rsqrt(jnp.mean(xf * xf, axis=-1, keepdims=True) + RMS_EPS)
    return (y * g.astype(jnp.float32)).astype(x.dtype)

def pool_mixer(u, w_pool, pool_scale):
    b, s, _ = u.shape
    ug = u.reshape(b, s, N_POOL_GROUPS, POOL_GROUP_W)
    cs = jnp.cumsum(ug.astype(jnp.float32), axis=1)
    pos = jnp.arange(1, s + 1, dtype=jnp.float32)
    outs = []
    for g, w in enumerate(POOL_WINDOWS):
        c = cs[:, :, g]
        prev = jnp.pad(c, ((0, 0), (w, 0), (0, 0)))[:, :s]
        cnt = jnp.minimum(pos, float(w))[None, :, None]
        outs.append((c - prev) / cnt - ug[:, :, g].astype(jnp.float32))
    d = jnp.stack(outs, axis=2).astype(u.dtype)
    y = jnp.einsum('bsgc,gcd->bsgd', d, w_pool).reshape(b, s, POOL_W)
    return y * pool_scale

def gated_short_conv(gb, gc, v, conv_w):
    z = gc * v
    rhs = conv_w[:, None, :]
    zc = lax.conv_general_dilated(z, rhs, window_strides=(1,), padding=[(CONV_K - 1, 0)],
                                  dimension_numbers=('NWC', 'WIO', 'NWC'),
                                  feature_group_count=CONV_W)
    return gb * zc

def mem_cross_attention(hn, mn, w_q, w_k, w_v, w_o):
    b, s, _ = hn.shape
    m = mn.shape[1]
    q = (hn @ w_q).reshape(b, s, N_XHEADS, XHEAD_DIM)
    k = (mn @ w_k).reshape(b, m, N_XHEADS, XHEAD_DIM)
    v = (mn @ w_v).reshape(b, m, N_XHEADS, XHEAD_DIM)
    sc = jnp.einsum('bshd,bmhd->bhsm', q, k).astype(jnp.float32) * (XHEAD_DIM ** -0.5)
    p = jax.nn.softmax(sc, axis=-1).astype(v.dtype)
    o = jnp.einsum('bhsm,bmhd->bshd', p, v).reshape(b, s, D_MODEL)
    return o @ w_o

def routed_experts(hn, w_router, b_router, w_gate_up, b_gate_up, w_down, b_down):
    b, s, d = hn.shape
    t = b * s
    xt = hn.reshape(t, d)
    logits = xt.astype(jnp.float32) @ w_router.astype(jnp.float32) + b_router.astype(jnp.float32)
    top_val, top_idx = lax.top_k(logits, TOP_K)
    gates = jax.nn.softmax(top_val, axis=-1)
    a = t * TOP_K
    flat_e = top_idx.reshape(a).astype(jnp.int32)
    flat_tok = jnp.repeat(jnp.arange(t, dtype=jnp.int32), TOP_K)
    flat_gate = gates.reshape(a)
    order = jnp.argsort(flat_e)
    sorted_e = flat_e[order]
    counts = jnp.bincount(flat_e, length=N_EXPERTS).astype(jnp.int32)
    starts = jnp.cumsum(counts) - counts
    padded = ((counts + EXPERT_BLOCK - 1) // EXPERT_BLOCK) * EXPERT_BLOCK
    pstarts = jnp.cumsum(padded) - padded
    rank = jnp.arange(a, dtype=jnp.int32) - starts[sorted_e]
    dest = pstarts[sorted_e] + rank
    p_len = a + N_EXPERTS * EXPERT_BLOCK
    n_blocks = p_len // EXPERT_BLOCK
    tok_buf = jnp.zeros((p_len,), jnp.int32).at[dest].set(flat_tok[order])
    gate_buf = jnp.zeros((p_len,), jnp.float32).at[dest].set(flat_gate[order])
    block_start = jnp.arange(n_blocks, dtype=jnp.int32) * EXPERT_BLOCK
    block_e = jnp.clip(jnp.searchsorted(pstarts, block_start, side='right') - 1, 0, N_EXPERTS - 1).astype(jnp.int32)

    def block_step(acc, blk):
        tok, g, e = blk
        xb = xt[tok]
        gu = xb @ w_gate_up[e] + b_gate_up[e]
        x_glu = jnp.minimum(gu[:, :D_FF], SWIGLU_LIMIT)
        x_lin = jnp.clip(gu[:, D_FF:], -SWIGLU_LIMIT, SWIGLU_LIMIT)
        act = (x_lin + 1) * (x_glu * jax.nn.sigmoid(SWIGLU_ALPHA * x_glu))
        y = act @ w_down[e] + b_down[e]
        acc = acc.at[tok].add((y.astype(jnp.float32) * g[:, None]).astype(acc.dtype))
        return acc, None

    acc, _ = lax.scan(block_step, jnp.zeros_like(xt),
                      (tok_buf.reshape(n_blocks, EXPERT_BLOCK),
                       gate_buf.reshape(n_blocks, EXPERT_BLOCK), block_e))
    return acc.reshape(b, s, d)

def setup_inputs(seed: int = 0) -> dict:
    key = jax.random.key(seed)
    ks = jax.random.split(key, 24)
    f32 = jnp.float32
    nrm = lambda k, shape, scale: jax.random.normal(k, shape, f32) * scale
    gain = lambda k, shape: 1.0 + 0.05 * jax.random.normal(k, shape, f32)
    L = DEPTH
    return {
        "x": jax.random.normal(ks[0], (BATCH, SEQ, D_MODEL), f32),
        "mem": jax.random.normal(ks[1], (BATCH, MEM_LEN, D_MODEL), f32),
        "g_mix": gain(ks[2], (L, D_MODEL)),
        "w_in": nrm(ks[3], (L, D_MODEL, IN_PROJ_W), D_MODEL ** -0.5),
        "w_pool": nrm(ks[4], (L, N_POOL_GROUPS, POOL_GROUP_W, POOL_GROUP_W), POOL_GROUP_W ** -0.5),
        "pool_scale": 1.0 + 0.1 * jax.random.normal(ks[5], (L, POOL_W), f32),
        "conv_w": nrm(ks[6], (L, CONV_K, CONV_W), CONV_K ** -0.5),
        "w_out": nrm(ks[7], (L, MIX_W, D_MODEL), MIX_W ** -0.5),
        "g_xattn": gain(ks[8], (L, D_MODEL)),
        "g_mem": gain(ks[9], (L, D_MODEL)),
        "w_q": nrm(ks[10], (L, D_MODEL, D_MODEL), D_MODEL ** -0.5),
        "w_k": nrm(ks[11], (L, D_MODEL, D_MODEL), D_MODEL ** -0.5),
        "w_v": nrm(ks[12], (L, D_MODEL, D_MODEL), D_MODEL ** -0.5),
        "w_o": nrm(ks[13], (L, D_MODEL, D_MODEL), D_MODEL ** -0.5),
        "g_moe": gain(ks[14], (L, D_MODEL)),
        "w_router": nrm(ks[15], (L, D_MODEL, N_EXPERTS), D_MODEL ** -0.5),
        "b_router": nrm(ks[16], (L, N_EXPERTS), 0.01),
        "w_gate_up": nrm(ks[17], (L, N_EXPERTS, D_MODEL, 2 * D_FF), D_MODEL ** -0.5),
        "b_gate_up": nrm(ks[18], (L, N_EXPERTS, 2 * D_FF), 0.01),
        "w_down": nrm(ks[19], (L, N_EXPERTS, D_FF, D_MODEL), D_FF ** -0.5),
        "b_down": nrm(ks[20], (L, N_EXPERTS, D_MODEL), 0.01),
        "g_final": gain(ks[21], (D_MODEL,)),
    }

def reference(x, mem, g_mix, w_in, w_pool, pool_scale, conv_w, w_out,
              g_xattn, g_mem, w_q, w_k, w_v, w_o,
              g_moe, w_router, b_router, w_gate_up, b_gate_up, w_down, b_down,
              g_final):
    h = x
    for l in range(DEPTH):
        hn = rmsnorm(h, g_mix[l])
        proj = hn @ w_in[l]
        u = proj[..., :POOL_W]
        gb = proj[..., POOL_W:POOL_W + CONV_W]
        gc = proj[..., POOL_W + CONV_W:POOL_W + 2 * CONV_W]
        v = proj[..., POOL_W + 2 * CONV_W:]
        y_pool = pool_mixer(u, w_pool[l], pool_scale[l])
        y_conv = gated_short_conv(gb, gc, v, conv_w[l])
        h = h + jnp.concatenate([y_pool, y_conv], axis=-1) @ w_out[l]
        h = h + mem_cross_attention(rmsnorm(h, g_xattn[l]), rmsnorm(mem, g_mem[l]),
                                    w_q[l], w_k[l], w_v[l], w_o[l])
        h = h + routed_experts(rmsnorm(h, g_moe[l]), w_router[l], b_router[l],
                               w_gate_up[l], b_gate_up[l], w_down[l], b_down[l])
    return rmsnorm(h, g_final)


_drawn_inputs = setup_inputs


def setup_inputs(seed=0):
    import zlib

    import numpy as np

    out = dict(_drawn_inputs(seed))
    spreads = {}
    factors = {'g_xattn': 3.219,
     'g_mem': 4.112,
     'b_gate_up': 35.745,
     'b_down': 40.721,
     'g_moe': 2.812,
     'b_router': 7.214}
    for name, (base, spread) in spreads.items():
        noise = np.random.default_rng([zlib.crc32(name.encode()), seed]).standard_normal(out[name].shape)
        drawn = base * np.exp(spread * noise) if base else spread * noise
        out[name] = __import__('jax').numpy.asarray(drawn.astype(out[name].dtype))
    for name, factor in factors.items():
        out[name] = (out[name] * factor).astype(out[name].dtype)
    return out
```

```python
from contextlib import ExitStack

import numpy as np

import concourse.bass as bass
from concourse import mybir

F32 = mybir.dt.float32
I32 = mybir.dt.int32
ALU = mybir.AluOpType
ACT = mybir.ActivationFunctionType
AX = mybir.AxisListType

P = 128
D = 1024
KC = D // P
SEQ = 256
TC = SEQ // P
HALF = 512
GROUPS = 4
WINDOWS = (2, 4, 8, 16)
PAD = max(WINDOWS)
CONV_K = 3
HEADS = 4
HEAD_DIM = D // HEADS
E = 32
TOP_K = 4
CAP = 64
ROUNDS = SEQ // CAP
LIMIT = 7.0
ALPHA = 1.702
EPS = 1e-5
FAR = 1e30

RING = 16
CHUNK = 2048
UNROLL = 4
PER_EXPERT = 12
W_IN_ORDER = (0, 1, 4, 6, 2, 5, 7, 3)
FRONT = 8 + 5 * 4

ROW_MIX, ROW_XATTN, ROW_MEM, ROW_MOE, ROW_POOL, ROW_CONV = 0, 8, 16, 24, 32, 36
N_ROWS = 48

A_USES = ["u0", "u1", "C0", "v0", "B0", "C1", "v1", "B1", "k0", "pool0", "k1", "pool1", "k2", "k3",
          "q0", "s0", "q1", "s1", "q2", "s2", "q3", "s3", "o0", "o1", "o2", "o3", "logits"]
T_USES = [["x0", "x2", "mem0", "mem2", "h0", "h2", "P0", "P2", "g0", "g2", "route"],
          ["vec", "x1", "x3", "mem1", "mem3", "h1", "h3", "P1", "P3", "g1", "g3"]]


def a_use(name):
    return A_USES.index(name)


def t_use(name):
    b = 0 if name in T_USES[0] else 1
    return b, T_USES[b].index(name) + 1


def program(nc, x, mem, g_mix, w_in, w_pool, pool_scale, conv_w, w_out, g_xattn, g_mem, w_q, w_k,
            w_v, w_o, g_moe, w_router, b_router, w_gate_up, b_gate_up, w_down, b_down, g_final, out):
    with ExitStack() as ctx:
        def sb(name, shape, dt=F32):
            return ctx.enter_context(nc.sbuf_tensor(name, shape, dt))

        def sem(name):
            return ctx.enter_context(nc.semaphore(name))

        ring = sb("ring", [P, RING, CHUNK])
        h_rows = sb("h_rows", [P, TC, D])
        n_rows = sb("n_rows", [P, TC, D])
        hnT = sb("hnT", [P, KC, SEQ])
        mem_rows = sb("mem_rows", [P, TC, D])
        mnT = sb("mnT", [P, KC, SEQ])
        kT = sb("kT", [P, KC, SEQ])
        v_rows = sb("v_rows", [P, TC, D])
        mixT = sb("mixT", [P, KC, SEQ])
        c_buf = sb("c_buf", [P, 2, SEQ])
        z_pad = sb("z_pad", [P, 2, 2 + SEQ])
        z_acc = sb("z_acc", [P, SEQ])
        ident = sb("ident", [P, P])
        tri = sb("tri", [P, P])
        ones = sb("ones", [P, P])
        slot_no = sb("slot_no", [P, CAP])
        count_r = sb("count_r", [P, PAD])
        vec_rows = sb("vec_rows", [N_ROWS, P])
        vec = sb("vec", [P, N_ROWS])
        wp_sb = sb("wp_sb", [P, GROUPS, P])
        wr_sb = sb("wr_sb", [P, KC, E])
        br_sb = sb("br_sb", [P, E])
        stat = sb("stat", [P, 5, TC])
        warm = sb("warm", [P, 1])
        smax = sb("smax", [P, 4, HEADS, TC])
        logT = sb("logT", [E, SEQ])
        lg = sb("lg", [P, TC, E + 8])
        top = sb("top", [P, TC, 8])
        marked = sb("marked", [P, TC, E + 8])
        mask = sb("mask", [P, TC, E])
        ex = sb("ex", [P, TC, E])
        small = sb("small", [P, 3, TC])
        gate = sb("gate", [P, TC, E + 1])
        place = sb("place", [P, TC, E + 1])
        cnt_i = sb("cnt_i", [1, E], I32)
        most_f = sb("most_f", [1, 1])
        most_i = sb("most_i", [1, 1], I32)

        def flat(t):
            return t[:].rearrange("p a b -> p (a b)")

        u_pad = flat(v_rows)[:, 0:GROUPS * (PAD + SEQ)].rearrange("p (g t) -> p g t", g=GROUPS)
        win = [flat(v_rows)[:, 1088 + 272 * i:1360 + 272 * i] for i in range(2)]
        early = flat(v_rows)[:, 1632:1632 + PAD]
        qT = mixT
        probs = flat(mem_rows).rearrange("p (c h m) -> p c h m", c=TC, h=HEADS)
        probsT = flat(mnT).rearrange("p (h c t) -> p h c t", h=HEADS, c=TC)
        oT = hnT
        xg_sb = flat(mem_rows)[:, 0:512]
        xT = [flat(mem_rows)[:, 512 * (1 + i):512 * (2 + i)] for i in range(2)]
        g_sb = flat(mem_rows)[:, 1536:1792]
        glu, lin, sig, act = (flat(mnT)[:, 512 * i:512 * (i + 1)] for i in range(4))
        bgu_sb = flat(kT)[0:E, :]
        actT = flat(v_rows)[:, 0:512]
        y_sb = flat(v_rows)[:, 512:1024]
        gfin = flat(v_rows)[:, 1024:2048]
        bdn_sb = flat(mixT)[0:E, 0:D]
        sel = flat(mixT)[:, 1024:1152].rearrange("p (c s) -> p c s", c=TC)
        selg = [flat(mixT)[:, 1152 + 256 * i:1408 + 256 * i].rearrange("p (c d s) -> p c d s", c=TC, d=2)
                for i in range(2)]
        onehot = [flat(mixT)[0:E, 1664 + 64 * i:1728 + 64 * i] for i in range(2)]

        ps = ctx.enter_context(nc.psum_tensor("ps", [P, 8, HALF], F32))
        bank_row = (2, 3, 4, 5)
        bank_t = (6, 7)
        bank_xg, bank_y = 2, 3

        slot_full = [sem(f"slot_full{i}") for i in range(RING)]
        x_in = [sem("x_in0"), sem("x_in1")]
        mem_in, vec_in, wp_in, wr_in, br_in, bgu_in, bdn_in, gfin_in = (
            sem(n) for n in ("mem_in", "vec_in", "wp_in", "wr_in", "br_in", "bgu_in", "bdn_in", "gfin_in"))
        chunks_used = sem("chunks_used")
        cleared, consts = sem("cleared"), sem("consts")
        a_full, a_free = sem("a_full"), [sem("a_free0"), sem("a_free1")]
        t_full, t_free = [sem("t_full0"), sem("t_full1")], [sem("t_free0"), sem("t_free1")]
        row_full, row_free = sem("row_full"), sem("row_free")
        squares, root, scaled = sem("squares"), sem("root"), sem("scaled")
        var_ready = sem("var_ready")
        mixed = sem("mixed")
        pooled = sem("pooled")
        c_done, z_used = sem("c_done"), sem("z_used")
        h_added = sem("h_added")
        neg_max, exps, probs_ok = sem("neg_max"), sem("exps"), sem("probs_ok")
        log_rows, route_neg, route_exp, masked = sem("log_rows"), sem("route_neg"), sem("route_exp"), sem("masked")
        rstd_ok = sem("rstd_ok")
        warmed = sem("warmed")
        ranked, routed = sem("ranked"), sem("routed")
        link = sem("link")
        step_link = sem("step_link")
        onehot_ok, sel_ok, selg_ok = sem("onehot_ok"), sem("sel_ok"), sem("selg_ok")
        xg_full, xg_ok, xT_full, xT_ok = sem("xg_full"), sem("xg_ok"), sem("xT_full"), sem("xT_ok")
        gT_full, g_ok = sem("gT_full"), sem("g_ok")
        glu_ok, sig_ok, act_ok = sem("glu_ok"), sem("sig_ok"), sem("act_ok")
        aT_full, aT_ok, y_ok = sem("aT_full"), sem("aT_ok"), sem("y_ok")
        sc_full, sc_added = sem("sc_full"), sem("sc_added")
        end_squares, end_link, stored = sem("end_squares"), sem("end_link"), sem("stored")
        end_var, end_root, end_out = sem("end_var"), sem("end_root"), sem("end_out")

        block = ctx.enter_context(nc.Block())

        def columns(w, c):
            return w[0].rearrange("(k p) n -> p k n", p=P)[:, :, 256 * c:256 * (c + 1)]

        def rows(w, c):
            return w[0, 256 * c:256 * (c + 1), :].rearrange("(a p) n -> p a n", p=P)

        front = [("w_in", columns(w_in, b)) for b in W_IN_ORDER]
        front += [("w_k", columns(w_k, c)) for c in range(4)]
        front += [("w_out", rows(w_out, c)) for c in range(4)]
        front += [("w_v", rows(w_v, c)) for c in range(4)]
        front += [("w_q", columns(w_q, c)) for c in range(4)]
        front += [("w_o", rows(w_o, c)) for c in range(4)]
        first = {name: [n for n, _ in front].index(name) for name in ("w_in", "w_k", "w_out", "w_v", "w_q", "w_o")}
        assert len(front) == FRONT and UNROLL * PER_EXPERT % RING == 0

        def chunk(q):
            return ring[:, q % RING, :]

        def full(eng, q):
            eng.wait_ge(slot_full[q % RING], 16 * (q // RING + 1))

        others = [n for n in A_USES if n[0] not in "uCvBkq"]
        chunk_of = {n: first["w_in"] + i for i, n in enumerate(("u0", "u1", "C0", "v0", "B0", "C1", "v1", "B1"))}
        chunk_of.update({f"{m}{h}": first[f"w_{m}"] + h for m in "kq" for h in range(4)})

        def a_complete(eng, name):
            if name in chunk_of:
                eng.wait_ge(chunks_used, chunk_of[name] + 1)
            else:
                eng.wait_ge(a_full, others.index(name) + 1)
            return ps[:, a_use(name) % 2, :], a_free[a_use(name) % 2]

        def row_complete(eng, use, r):
            if r < 3:
                eng.wait_ge(row_full, 3 * ("w_out", "w_v", "w_o").index(use) + r + 1)
            else:
                eng.wait_ge(chunks_used, first[use] + 4)

        total = FRONT + E * PER_EXPERT

        def expert_source(e, c):
            if c < 8:
                return w_gate_up[0, bass.ds(e, 1), P * c:P * (c + 1), :].rearrange("o p n -> p (o n)")
            return w_down[0, bass.ds(e, 1), 256 * (c - 8):256 * (c - 7), :].rearrange("o (a p) n -> p (o a) n", p=P)

        def expert_target(slot, c):
            return ring[:, slot, :] if c < 8 else ring[:, slot, :].rearrange("p (a n) -> p a n", a=2)

        def more_rounds(eng, body):
            k_reg = eng.alloc_register(f"rounds_{eng.engine.name}")
            eng.reg_mov(k_reg, 0)
            eng.wait_ge(routed, 1)
            with eng.If(eng.value_load(most_i[0:1, 0:1], min_val=0, max_val=SEQ) > CAP):
                for b in range(1, ROUNDS):
                    with eng.Fori(0, E) as e:
                        with eng.If(eng.value_load(cnt_i[0:1, bass.ds(e, 1)], min_val=0, max_val=SEQ) > CAP * b):
                            k = eng.snap(k_reg, min_val=0, max_val=SEQ * TOP_K // CAP)
                            body(b, e, k)
                            eng.reg_add(k_reg, k_reg, 1)
            return eng.snap(k_reg, min_val=0, max_val=SEQ * TOP_K // CAP)

        @block.sync
        def _(sp):
            for c in range(TC):
                sp.dma_start(h_rows[:, c, :], x[0, P * c:P * (c + 1), :]).then_inc(x_in[c], 16)
            for q, (_, src) in enumerate(front):
                if q == 2:
                    sp.dma_start(mem_rows[:], mem[0].rearrange("(c p) d -> p c d", p=P)).then_inc(mem_in, 16)
                if q >= RING:
                    sp.wait_ge(chunks_used, q - RING + 1)
                dst = chunk(q).rearrange("p (k n) -> p k n", k=src.shape[1])
                sp.dma_start(dst, src).then_inc(slot_full[q % RING], 16)
            with sp.Fori(0, E // UNROLL) as turn:
                e0 = turn * UNROLL
                for i in range(UNROLL * PER_EXPERT):
                    sp.wait_ge(chunks_used, e0 * PER_EXPERT + (FRONT + i - RING + 1))
                    slot = (FRONT + i) % RING
                    sp.dma_start(expert_target(slot, i % PER_EXPERT),
                                 expert_source(e0 + i // PER_EXPERT, i % PER_EXPERT)).then_inc(slot_full[slot], 16)

            def load_again(b, e, k):
                sp.wait_ge(chunks_used, k * PER_EXPERT + total)
                for c in range(PER_EXPERT):
                    sp.dma_start(expert_target(c, c), expert_source(e, c)).then_inc(slot_full[c], 16)
            more_rounds(sp, load_again)
            for c in range(TC):
                sp.wait_ge(end_out, c + 1)
                sp.dma_start(out[0, P * c:P * (c + 1), :], n_rows[:, c, :]).then_inc(stored, 16)
            sp.wait_ge(stored, 16 * TC)

        @block.gpsimd
        def _(pool):
            pool.memset(ident[:], 0.0).then_inc(cleared, 1)
            pool.memset(tri[:], 1.0).then_inc(cleared, 1)
            pool.wait_ge(cleared, 2)
            pool.affine_select(out=ident[:], in_=ident[:], compare_op=ALU.not_equal, fill=1.0, base=0,
                               pattern=[[-1, P]], channel_multiplier=1).then_inc(consts, 1)
            pool.affine_select(out=tri[:], in_=tri[:], compare_op=ALU.is_gt, fill=0.0, base=0,
                               pattern=[[1, P]], channel_multiplier=-1).then_inc(consts, 1)
            pool.memset(ones[:], 1.0).then_inc(consts, 1)
            pool.memset(u_pad[:, :, 0:PAD], 0.0).then_inc(consts, 1)
            pool.memset(z_pad[:, :, 0:2], 0.0).then_inc(consts, 1)
            pool.iota(count_r[:], pattern=[[1, PAD]], base=1, channel_multiplier=0,
                      allow_small_or_imprecise_dtypes=True).then_inc(consts, 1)
            pool.iota(slot_no[:], pattern=[[1, CAP]], base=1, channel_multiplier=0,
                      allow_small_or_imprecise_dtypes=True).then_inc(consts, 1)
            pool.memset(gate[:, :, E:E + 1], 0.0).then_inc(consts, 1)
            pool.memset(place[:, :, E:E + 1], 0.0).then_inc(consts, 1)
            pool.memset(lg[:, :, E:E + 8], -FAR).then_inc(consts, 1)
            pool.dma_start(wp_sb[:], w_pool[0].rearrange("g c d -> c g d")).then_inc(wp_in, 16)
            pool.dma_start(br_sb[:], b_router[0].partition_broadcast(P)).then_inc(br_in, 16)
            pool.dma_start(wr_sb[:], w_router[0].rearrange("(k p) e -> p k e", p=P)).then_inc(wr_in, 16)
            a_complete(pool, "s3")
            pool.dma_start(bgu_sb, b_gate_up[0]).then_inc(bgu_in, 16)
            pool.dma_start(bdn_sb, b_down[0]).then_inc(bdn_in, 16)
            a_complete(pool, "o3")
            pool.dma_start(gfin, g_final.partition_broadcast(P)).then_inc(gfin_in, 16)
        N_CONSTS = 10

        @block.tensor
        def _(pe):
            def t_begin(name):
                b, n = t_use(name)
                if n > 1:
                    pe.wait_ge(t_free[b], n - 1)
                return ps[:, bank_t[b], :], t_full[b]

            def transpose_rows(name, src, pair):
                bank, done = t_begin(f"{name}{pair}")
                for c in range(2):
                    for t in range(TC):
                        k = 2 * pair + c
                        mm = pe.transpose(bank[:, c * SEQ + t * P:c * SEQ + (t + 1) * P],
                                          src[:, t, k * P:(k + 1) * P], ident[:])
                mm.then_inc(done, 1)

            def a_begin(name):
                n = a_use(name)
                if n >= 2:
                    pe.wait_ge(a_free[n % 2], n // 2)
                return ps[:, n % 2, :]

            def project_columns(name, q, src):
                bank = a_begin(name)
                full(pe, q)
                w = chunk(q).rearrange("p (k n) -> p k n", k=KC)
                for f in range(2):
                    for k in range(KC):
                        mm = pe.matmul(bank[:, f * SEQ:(f + 1) * SEQ], w[:, k, f * P:(f + 1) * P], src[:, k, :],
                                       start=(k == 0), stop=(k == KC - 1), skip_group_check=True)
                mm.then_inc(chunks_used, 1)

            def project_rows(q0, c, srcT):
                full(pe, q0 + c)
                w = chunk(q0 + c).rearrange("p (a n) -> p a n", a=2)
                for r in range(4):
                    t, half = r // 2, r % 2
                    for a in range(2):
                        k = 2 * c + a
                        mm = pe.matmul(ps[:, bank_row[r], :], srcT[:, k, t * P:(t + 1) * P],
                                       w[:, a, half * HALF:(half + 1) * HALF], start=(k == 0), stop=(k == KC - 1),
                                       skip_group_check=True)
                    if c == 3 and r < 3:
                        mm.then_inc(row_full, 1)
                mm.then_inc(chunks_used, 1)

            pe.wait_ge(consts, 1)
            pe.wait_ge(vec_in, 16 * 6)
            bank, done = t_begin("vec")
            pe.transpose(bank[:, 0:N_ROWS], vec_rows[:], ident[0:N_ROWS, 0:N_ROWS]).then_inc(done, 1)
            pe.wait_ge(scaled, 1)
            for pair in range(4):
                transpose_rows("x", n_rows, pair)
            for i, name in enumerate(("u0", "u1", "C0", "v0", "B0", "C1", "v1", "B1")):
                if i == 0:
                    pe.wait_ge(t_free[0], t_use("x2")[1])
                    pe.wait_ge(t_free[1], t_use("x3")[1])
                project_columns(name, first["w_in"] + i, hnT)
                if i == 1:
                    pe.wait_ge(scaled, 2)
                    for pair in range(4):
                        transpose_rows("mem", mem_rows, pair)

            def pool_product(i):
                bank = a_begin(f"pool{i}")
                pe.wait_ge(pooled, 2 * (i + 1))
                if i == 0:
                    pe.wait_ge(wp_in, 16)
                for g in range(2):
                    mm = pe.matmul(bank[:, g * SEQ:(g + 1) * SEQ], wp_sb[:, 2 * i + g, :], u_pad[:, 2 * i + g, PAD:],
                                   start=True, stop=True, skip_group_check=True)
                mm.then_inc(a_full, 1)

            pe.wait_ge(t_free[0], t_use("mem2")[1])
            pe.wait_ge(t_free[1], t_use("mem3")[1])
            for c in range(4):
                project_columns(f"k{c}", first["w_k"] + c, mnT)
                if c < 2:
                    pool_product(c)
            pe.wait_ge(mixed, 8)
            for c in range(4):
                project_rows(first["w_out"], c, mixT)
            for c in range(4):
                if c == 0:
                    pe.wait_ge(row_free, 4)
                project_rows(first["w_v"], c, mnT)
            pe.wait_ge(scaled, 3)
            for pair in range(4):
                transpose_rows("h", n_rows, pair)
            pe.wait_ge(t_free[0], t_use("h2")[1])
            pe.wait_ge(t_free[1], t_use("h3")[1])

            def query(h):
                project_columns(f"q{h}", first["w_q"] + h, hnT)

            def scores(h):
                bank = a_begin(f"s{h}")
                pe.wait_ge(a_free[a_use(f"q{h}") % 2], a_use(f"q{h}") // 2 + 1)
                if h == 0:
                    pe.wait_ge(a_free[a_use("k3") % 2], a_use("k3") // 2 + 1)
                    pe.wait_ge(a_free[a_use("k2") % 2], a_use("k2") // 2 + 1)
                for t in range(TC):
                    for a in range(2):
                        mm = pe.matmul(bank[:, t * SEQ:(t + 1) * SEQ], qT[:, 2 * h + a, t * P:(t + 1) * P],
                                       kT[:, 2 * h + a, :], start=(a == 0), stop=(a == 1), skip_group_check=True)
                mm.then_inc(a_full, 1)

            def turn_probs(h):
                bank, done = t_begin(f"P{h}")
                pe.wait_ge(probs_ok, h + 1)
                for m in range(TC):
                    for t in range(TC):
                        mm = pe.transpose(bank[:, m * SEQ + t * P:m * SEQ + (t + 1) * P],
                                          probs[:, t, h, m * P:(m + 1) * P], ident[:])
                mm.then_inc(done, 1)

            def attend(h):
                bank = a_begin(f"o{h}")
                b, n = t_use(f"P{h}")
                pe.wait_ge(t_free[b], n)
                if h == 0:
                    pe.wait_ge(row_free, 8)
                for f in range(2):
                    for m in range(TC):
                        mm = pe.matmul(bank[:, f * SEQ:(f + 1) * SEQ],
                                       v_rows[:, m, (2 * h + f) * P:(2 * h + f + 1) * P], probsT[:, h, m, :],
                                       start=(m == 0), stop=(m == TC - 1), skip_group_check=True)
                mm.then_inc(a_full, 1)

            def project_head(h):
                n = a_use(f"o{h}")
                pe.wait_ge(a_free[n % 2], n // 2 + 1)
                project_rows(first["w_o"], h, oT)

            query(0), scores(0), query(1), scores(1), turn_probs(0)
            query(2), scores(2), turn_probs(1)
            query(3), scores(3), attend(0), turn_probs(2), attend(1)
            project_head(0), attend(2)
            project_head(1), turn_probs(3), attend(3)
            project_head(2), project_head(3)
            pe.wait_ge(h_added, 8)
            for pair in range(4):
                transpose_rows("g", h_rows, pair)
            pe.wait_ge(t_free[0], t_use("g2")[1])
            pe.wait_ge(t_free[1], t_use("g3")[1])
            pe.wait_ge(wr_in, 16)
            bank = a_begin("logits")
            for k in range(KC):
                mm = pe.matmul(bank[0:E, 0:SEQ], wr_sb[:, k, :], hnT[:, k, :], start=(k == 0), stop=(k == KC - 1))
            mm.then_inc(a_full, 1)
            bank, done = t_begin("route")
            n = a_use("logits")
            pe.wait_ge(a_free[n % 2], n // 2 + 1)
            for t in range(TC):
                mm = pe.transpose(bank[:, t * E:(t + 1) * E], logT[:, t * P:(t + 1) * P], ident[0:E, 0:E])
            mm.then_inc(done, 1)
            pe.wait_ge(masked, TC)
            pe.wait_ge(consts, N_CONSTS)
            bank = ps[:, 0, :]
            pe.matmul(bank[:, 0:E], tri[:], mask[:, 0, :], start=True, stop=True, skip_group_check=True)
            pe.matmul(bank[:, E:2 * E], ones[:], mask[:, 0, :], start=True, stop=False, skip_group_check=True)
            pe.matmul(bank[:, E:2 * E], tri[:], mask[:, 1, :], start=False, stop=True, skip_group_check=True)
            pe.matmul(bank[:, 2 * E:3 * E], ones[:], mask[:, 0, :], start=True, stop=False, skip_group_check=True)
            pe.matmul(bank[:, 2 * E:3 * E], ones[:], mask[:, 1, :], start=False, stop=True,
                      skip_group_check=True).then_inc(ranked, 1)

            def gather(s):
                pe.wait_ge(sel_ok, s + 1)
                for t in range(TC):
                    for half in range(2):
                        mm = pe.matmul(ps[CAP * half:CAP * (half + 1), bank_xg, :], sel[:, t, :],
                                       n_rows[:, t, half * HALF:(half + 1) * HALF], start=(t == 0), stop=(t == TC - 1),
                                       skip_group_check=True)
                mm.then_inc(xg_full, 1)

            def turn_tokens(s):
                pe.wait_ge(xg_ok, s + 1)
                for j in range(4):
                    mm = pe.transpose(ps[:, bank_t[0], j * P:(j + 1) * P], xg_sb[:, j * P:(j + 1) * P], ident[:])
                mm.then_inc(xT_full, 1)

            def gate_up(s, par, wait_chunk, ahead=1):
                pe.wait_ge(xT_ok, s + ahead)
                pe.wait_ge(onehot_ok, s + ahead)
                for bank in range(2):
                    for half in range(2):
                        pe.matmul(ps[CAP * half:CAP * (half + 1), bank, :], onehot[par],
                                  bgu_sb[:, bank * D + half * HALF:bank * D + (half + 1) * HALF], start=True, stop=False,
                                  skip_group_check=True)
                for k in range(KC):
                    w = wait_chunk(k)
                    lhsT = xT[par][:, (k % 4) * P + CAP * (k // 4):(k % 4) * P + CAP * (k // 4 + 1)]
                    for bank in range(2):
                        for half in range(2):
                            mm = pe.matmul(ps[CAP * half:CAP * (half + 1), bank, :], lhsT,
                                           w[:, bank * D + half * HALF:bank * D + (half + 1) * HALF], start=False,
                                           stop=(k == KC - 1), skip_group_check=True)
                    mm.then_inc(chunks_used, 1)

            def turn_gates(s, par, ahead=1):
                pe.wait_ge(selg_ok, s + ahead)
                for t in range(TC):
                    mm = pe.transpose(ps[:, bank_t[1], t * P:(t + 1) * P],
                                      selg[par][:, t, :, :].rearrange("p d s -> p (d s)"), ident[:])
                mm.then_inc(gT_full, 1)

            def turn_act(s):
                pe.wait_ge(act_ok, s + 1)
                pe.wait_ge(g_ok, s + 1)
                for j in range(4):
                    mm = pe.transpose(ps[:, bank_t[1], j * P:(j + 1) * P], act[:, j * P:(j + 1) * P], ident[:])
                mm.then_inc(aT_full, 1)

            def down(s, par, wait_chunk):
                for half in range(2):
                    pe.matmul(ps[CAP * half:CAP * (half + 1), bank_y, :], onehot[par],
                              bdn_sb[:, half * HALF:(half + 1) * HALF], start=True, stop=False, skip_group_check=True)
                pe.wait_ge(aT_ok, s + 1)
                for c in range(8, PER_EXPERT):
                    w = wait_chunk(c)
                    for a in range(2):
                        k = 2 * (c - 8) + a
                        lhsT = actT[:, (k % 4) * P + CAP * (k // 4):(k % 4) * P + CAP * (k // 4 + 1)]
                        for half in range(2):
                            mm = pe.matmul(ps[CAP * half:CAP * (half + 1), bank_y, :], lhsT,
                                           w[:, a * D + half * HALF:a * D + (half + 1) * HALF], start=False,
                                           stop=(k == KC - 1), skip_group_check=True)
                    mm.then_inc(chunks_used, 1)

            def scatter(s):
                pe.wait_ge(y_ok, s + 1)
                for t in range(TC):
                    for half in range(2):
                        rws = slice(CAP * half, CAP * (half + 1))
                        mm = pe.matmul(ps[:, (4 if t == 0 else 2) + half, :], g_sb[rws, t * P:(t + 1) * P],
                                       y_sb[rws, :], start=True, stop=True, skip_group_check=True)
                    mm.then_inc(sc_full, 1)

            pe.wait_ge(scaled, 3 + TC)
            gather(0)
            turn_tokens(0)
            pe.wait_ge(bgu_in, 16)
            pe.wait_ge(bdn_in, 16)
            with pe.Fori(0, E // UNROLL) as turn:
                e0 = turn * UNROLL
                for u in range(UNROLL):
                    def ring_chunk(c, u=u):
                        q = FRONT + u * PER_EXPERT + c
                        uses = UNROLL * PER_EXPERT // RING
                        pe.wait_ge(slot_full[q % RING], e0 * (16 * uses // UNROLL) + 16 * (q // RING + 1))
                        return ring[:, q % RING, :]
                    s = e0 + u
                    gate_up(s, u % 2, ring_chunk)
                    gather(s + 1)
                    turn_gates(s, u % 2)
                    turn_tokens(s + 1)
                    turn_act(s)
                    down(s, u % 2, ring_chunk)
                    scatter(s)

            def again(b, e, k):
                s = k + E
                def ring_chunk(c):
                    uses = (total - 1 - c) // RING + 1
                    pe.wait_ge(slot_full[c], k * 16 + 16 * (uses + 1))
                    return ring[:, c, :]
                gather(s + 1)
                turn_tokens(s + 1)
                gate_up(s, 0, ring_chunk, ahead=2)
                turn_gates(s, 0, ahead=2)
                turn_act(s)
                down(s, 0, ring_chunk)
                scatter(s)

            more_rounds(pe, again)

        @block.scalar
        def _(act_e):
            rows_of = [(ROW_MIX, g_mix[0].rearrange("(c p) -> c p", p=P)),
                       (ROW_XATTN, g_xattn[0].rearrange("(c p) -> c p", p=P)),
                       (ROW_MEM, g_mem[0].rearrange("(c p) -> c p", p=P)),
                       (ROW_MOE, g_moe[0].rearrange("(c p) -> c p", p=P)),
                       (ROW_POOL, pool_scale[0].rearrange("(c p) -> c p", p=P)),
                       (ROW_CONV, conv_w[0].rearrange("k (c p) -> (k c) p", p=P))]
            for r, src in rows_of:
                act_e.dma_start(vec_rows[r:r + src.shape[0], :], src).then_inc(vec_in, 16)

            def copy(dst, src, done):
                act_e.activation(dst, src, ACT.Copy).then_inc(done, 1)

            def fetch_table(fn):
                fetched[0] += 1
                act_e.activation(warm[:], ones[:, 0:1], fn).then_inc(warmed, 1)
                act_e.wait_ge(warmed, fetched[0])
            fetched = [0]

            def squares_of(src, junk):
                for c in range(TC):
                    act_e.activation(junk[:, c, :], src[:, c, :], ACT.Square,
                                     accum_out=stat[:, 0, c:c + 1]).then_inc(squares, 1)

            def root_of(n):
                act_e.wait_ge(var_ready, n)
                act_e.activation(stat[:, 2, :], stat[:, 1, :], ACT.Sqrt).then_inc(root, 1)

            def t_out(name, fn):
                b, n = t_use(name)
                act_e.wait_ge(t_full[b], n)
                fn(ps[:, bank_t[b], :], t_free[b])

            def with_gain(dst, row, pair):
                def fn(bank, done):
                    for c in range(2):
                        k = 2 * pair + c
                        ins = act_e.activation(dst[:, k, :], bank[:, c * SEQ:(c + 1) * SEQ], ACT.Copy,
                                               scale=vec[:, row + k:row + k + 1])
                    ins.then_inc(done, 1)
                return fn

            def a_out(name, dst):
                bank, done = a_complete(act_e, name)
                copy(dst, bank.rearrange("p (a b) -> p a b", a=2), done)

            junk_x = mnT[:].rearrange("p (c k) t -> p c (k t)", c=TC)
            junk_mem = mixT[:].rearrange("p (c k) t -> p c (k t)", c=TC)
            for c in range(TC):
                act_e.wait_ge(x_in[c], 16)
                act_e.activation(junk_x[:, c, :], h_rows[:, c, :], ACT.Square,
                                 accum_out=stat[:, 0, c:c + 1]).then_inc(squares, 1)
            root_of(1)
            t_out("vec", lambda bank, done: copy(vec[:], bank[:, 0:N_ROWS], done))
            act_e.wait_ge(mem_in, 16)
            act_e.wait_ge(scaled, 1)
            squares_of(mem_rows, junk_mem)
            root_of(2)
            act_e.wait_ge(t_free[1], 1)
            t_out("x1", with_gain(hnT, ROW_MIX, 1))
            t_out("x3", with_gain(hnT, ROW_MIX, 3))
            a_out("u0", u_pad[:, 0:2, PAD:])
            a_out("u1", u_pad[:, 2:4, PAD:])
            t_out("mem1", with_gain(mnT, ROW_MEM, 1))
            t_out("mem3", with_gain(mnT, ROW_MEM, 3))
            for i in range(2):
                if i:
                    act_e.wait_ge(z_used, 1)
                a_out(f"C{i}", c_buf[:])
            for c in range(4):
                a_out(f"k{c}", kT[:, 2 * c:2 * c + 2, :])
            act_e.wait_ge(consts, N_CONSTS)
            act_e.wait_ge(h_added, 4)
            squares_of(h_rows, mem_rows)
            root_of(3)
            t_out("h1", with_gain(hnT, ROW_XATTN, 1))
            t_out("h3", with_gain(hnT, ROW_XATTN, 3))
            for r in range(4):
                row_complete(act_e, "w_v", r)
                copy(v_rows[:, r // 2, (r % 2) * HALF:(r % 2 + 1) * HALF], ps[:, bank_row[r], :], row_free)

            def softmax(h):
                n = a_use(f"s{h}")
                act_e.wait_ge(neg_max, h + 1)
                for t in range(TC):
                    ins = act_e.activation(probs[:, t, h, :], ps[:, n % 2, t * SEQ:(t + 1) * SEQ], ACT.Exp,
                                           bias=smax[:, 1, h, t:t + 1], scale=HEAD_DIM ** -0.5,
                                           accum_out=smax[:, 2, h, t:t + 1])
                    ins.then_inc(exps, 1)
                act_e.wait_ge(exps, TC * (h + 1))
                act_e.sem_inc(a_free[n % 2], 1)

            def out_head(h):
                a_out(f"o{h}", oT[:, 2 * h:2 * h + 2, :])

            def turned(h):
                t_out(f"P{h}", lambda bank, done: copy(probsT[:, h, :, :], bank.rearrange("p (c t) -> p c t", c=TC), done))
            a_out("q0", qT[:, 0:2, :]), softmax(0)
            a_out("q1", qT[:, 2:4, :]), softmax(1)
            a_out("q2", qT[:, 4:6, :]), softmax(2)
            turned(1)
            a_out("q3", qT[:, 6:8, :]), softmax(3)
            out_head(0), out_head(1), out_head(2)
            turned(3), out_head(3)
            act_e.wait_ge(h_added, 8)
            squares_of(h_rows, mem_rows)
            t_out("g1", with_gain(hnT, ROW_MOE, 1))
            root_of(4)
            t_out("g3", with_gain(hnT, ROW_MOE, 3))
            fetch_table(ACT.Exp)
            act_e.wait_ge(rstd_ok, 1)
            for c in range(TC):
                act_e.activation(n_rows[:, c, :], h_rows[:, c, :], ACT.Copy, scale=stat[:, 3, c:c + 1]).then_inc(scaled, 1)
            act_e.wait_ge(route_neg, 1)
            for t in range(TC):
                act_e.activation(ex[:, t, :], lg[:, t, 0:E], ACT.Exp, bias=small[:, 0, t:t + 1]).then_inc(route_exp, 1)

            def tokens_out(s):
                act_e.wait_ge(xg_full, s + 1)
                copy(xg_sb, ps[:, bank_xg, :], xg_ok)

            def sigmoid(s):
                act_e.wait_ge(glu_ok, s + 1)
                act_e.activation(sig, glu, ACT.Sigmoid, scale=ALPHA).then_inc(sig_ok, 1)

            def gates_out(s):
                act_e.wait_ge(gT_full, s + 1)
                copy(g_sb, ps[:, bank_t[1], 0:SEQ], g_ok)

            def act_out(s):
                act_e.wait_ge(aT_full, s + 1)
                copy(actT, ps[:, bank_t[1], :], aT_ok)

            def y_out(s):
                act_e.wait_ge(chunks_used, s * PER_EXPERT + (FRONT + PER_EXPERT))
                copy(y_sb, ps[:, bank_y, :], y_ok)

            fetch_table(ACT.Sigmoid)
            tokens_out(0)
            with act_e.Fori(0, E) as s:
                sigmoid(s)
                tokens_out(s + 1)
                gates_out(s)
                act_out(s)
                y_out(s)

            def again(b, e, k):
                s = k + E
                tokens_out(s + 1)
                sigmoid(s)
                gates_out(s)
                act_out(s)
                y_out(s)
            k = more_rounds(act_e, again)
            fetch_table(ACT.Sqrt)
            junk = mnT[:].rearrange("p (c k) t -> p c (k t)", c=TC)
            for c in range(TC):
                act_e.wait_ge(sc_added, k * TC + (E * TC - TC + c + 1))
                act_e.activation(junk[:, c, :], h_rows[:, c, :], ACT.Square,
                                 accum_out=stat[:, 0, c:c + 1]).then_inc(end_squares, 1)
            for c in range(TC):
                act_e.wait_ge(end_var, c + 1)
                act_e.activation(stat[:, 2, c:c + 1], stat[:, 1, c:c + 1], ACT.Sqrt).then_inc(end_root, 1)

        @block.vector
        def _(dve):
            links = [0]

            def linked(ins):
                links[0] += 1
                ins.then_inc(link, 1)
                dve.wait_ge(link, links[0])

            def of_tokens(c):
                return slice(0, TC) if c is None else slice(c, c + 1)

            def variance(c=None):
                t = of_tokens(c)
                return dve.tensor_scalar(stat[:, 1, t], stat[:, 0, t], 1.0 / D, EPS, ALU.mult, ALU.add)

            def newton(ln, c=None):
                t = of_tokens(c)
                ln(dve.reciprocal(stat[:, 3, t], stat[:, 2, t]))
                ln(dve.tensor_tensor(stat[:, 4, t], stat[:, 3, t], stat[:, 3, t], ALU.mult))
                ln(dve.tensor_tensor(stat[:, 4, t], stat[:, 4, t], stat[:, 1, t], ALU.mult))
                ln(dve.tensor_scalar(stat[:, 4, t], stat[:, 4, t], -0.5, 1.5, ALU.mult, ALU.add))
                ln(dve.tensor_tensor(stat[:, 3, t], stat[:, 3, t], stat[:, 4, t], ALU.mult))

            def normalise(n, src, dst):
                dve.wait_ge(squares, TC * n)
                variance().then_inc(var_ready, 1)
                dve.wait_ge(root, n)
                newton(linked)
                linked(dve.tensor_scalar(dst[:, 0, :], src[:, 0, :], stat[:, 3, 0:1], None, ALU.mult))
                dve.tensor_scalar(dst[:, 1, :], src[:, 1, :], stat[:, 3, 1:2], None, ALU.mult).then_inc(scaled, 1)
                dve.wait_ge(scaled, n)

            def t_with_gain(name, dst, row, pair):
                b, n = t_use(f"{name}{pair}")
                dve.wait_ge(t_full[b], n)
                gain = vec[:, row + 2 * pair:row + 2 * pair + 2].unsqueeze(2).broadcast_to([P, 2, SEQ])
                dve.tensor_tensor(dst[:, 2 * pair:2 * pair + 2, :],
                                  ps[:, bank_t[b], :].rearrange("p (c t) -> p c t", c=2), gain,
                                  ALU.mult).then_inc(t_free[b], 1)

            for c in range(TC):
                dve.wait_ge(x_in[c], 16)
            normalise(1, h_rows, n_rows)
            dve.wait_ge(t_free[1], 1)
            t_with_gain("x", hnT, ROW_MIX, 0)
            t_with_gain("x", hnT, ROW_MIX, 2)
            normalise(2, mem_rows, mem_rows)
            dve.wait_ge(consts, N_CONSTS)
            linked(dve.reciprocal(count_r[:], count_r[:]))
            t_with_gain("mem", mnT, ROW_MEM, 0)
            t_with_gain("mem", mnT, ROW_MEM, 2)
            for g, w in enumerate(WINDOWS):
                if g % 2 == 0:
                    n = a_use(f"u{g // 2}")
                    dve.wait_ge(a_free[n % 2], n // 2 + 1)
                src, span, buf = u_pad[:, g, :], 1, 0
                while span < w:
                    lo = 2 * span - 1
                    linked(dve.tensor_tensor(win[buf][:, lo:], src[:, lo:], src[:, lo - span:PAD + SEQ - span], ALU.add))
                    src, span, buf = win[buf], 2 * span, 1 - buf
                frame = u_pad[:, g, :]
                linked(dve.tensor_tensor(early[:, 0:w], src[:, PAD:PAD + w], count_r[:, 0:w], ALU.mult))
                linked(dve.tensor_tensor(frame[:, PAD:PAD + w], early[:, 0:w], frame[:, PAD:PAD + w], ALU.subtract))
                dve.scalar_tensor_tensor(out=frame[:, PAD + w:], in0=src[:, PAD + w:], scalar=1.0 / w,
                                         in1=frame[:, PAD + w:], op0=ALU.mult, op1=ALU.subtract).then_inc(pooled, 1)
                dve.wait_ge(pooled, g + 1)
            for i in range(2):
                n = a_use(f"C{i}")
                dve.wait_ge(a_free[n % 2], n // 2 + 1)
                bank, done = a_complete(dve, f"v{i}")
                dve.tensor_tensor(z_pad[:, :, 2:], bank.rearrange("p (a t) -> p a t", a=2), c_buf[:],
                                  ALU.mult).then_inc(done, 1)
                dve.wait_ge(done, a_use(f"v{i}") // 2 + 1)
                dve.sem_inc(z_used, 1)
                bank, done = a_complete(dve, f"B{i}")
                for a in range(2):
                    def tap(k):
                        r = ROW_CONV + GROUPS * k + 2 * i + a
                        return vec[:, r:r + 1]
                    linked(dve.tensor_scalar(z_acc[:], z_pad[:, a, 2:], tap(2), None, ALU.mult))
                    for k in (1, 0):
                        linked(dve.scalar_tensor_tensor(out=z_acc[:], in0=z_pad[:, a, k:k + SEQ], scalar=tap(k),
                                                        in1=z_acc[:], op0=ALU.mult, op1=ALU.add))
                    dve.tensor_tensor(mixT[:, 4 + 2 * i + a, :], bank[:, a * SEQ:(a + 1) * SEQ], z_acc[:],
                                      ALU.mult).then_inc(mixed, 1)
                    dve.wait_ge(mixed, 2 * i + a + 1)
                dve.sem_inc(done, 1)
            for i in range(2):
                bank, done = a_complete(dve, f"pool{i}")
                for a in range(2):
                    g = 2 * i + a
                    dve.tensor_scalar(mixT[:, g, :], bank[:, a * SEQ:(a + 1) * SEQ],
                                      vec[:, ROW_POOL + g:ROW_POOL + g + 1], None, ALU.mult).then_inc(mixed, 1)
                dve.wait_ge(mixed, 4 + 2 * i + 2)
                dve.sem_inc(done, 1)

            def add_rows(use):
                for r in range(4):
                    row_complete(dve, use, r)
                    part = h_rows[:, r // 2, (r % 2) * HALF:(r % 2 + 1) * HALF]
                    dve.tensor_tensor(part, ps[:, bank_row[r], :], part, ALU.add).then_inc(h_added, 1)
            add_rows("w_out")
            dve.wait_ge(h_added, 4)
            dve.sem_inc(row_free, 4)
            normalise(3, h_rows, n_rows)
            t_with_gain("h", hnT, ROW_XATTN, 0)
            t_with_gain("h", hnT, ROW_XATTN, 2)

            def largest(h):
                bank, _ = a_complete(dve, f"s{h}")
                linked(dve.tensor_reduce(smax[:, 0, h, :], bank.rearrange("p (c m) -> p c m", c=TC), AX.X, ALU.max))
                dve.tensor_scalar(smax[:, 1, h, :], smax[:, 0, h, :], -HEAD_DIM ** -0.5, None, ALU.mult).then_inc(neg_max, 1)

            def scale_probs(h):
                dve.wait_ge(exps, TC * (h + 1))
                linked(dve.reciprocal(smax[:, 3, h, :], smax[:, 2, h, :]))
                linked(dve.tensor_scalar(probs[:, 0, h, :], probs[:, 0, h, :], smax[:, 3, h, 0:1], None, ALU.mult))
                dve.tensor_scalar(probs[:, 1, h, :], probs[:, 1, h, :], smax[:, 3, h, 1:2], None, ALU.mult).then_inc(probs_ok, 1)

            def turned(h):
                b, n = t_use(f"P{h}")
                dve.wait_ge(t_full[b], n)
                dve.tensor_copy(probsT[:, h, :, :], ps[:, bank_t[b], :].rearrange("p (c t) -> p c t", c=TC)).then_inc(t_free[b], 1)
            largest(0), scale_probs(0), largest(1), scale_probs(1), turned(0)
            largest(2), scale_probs(2), largest(3), scale_probs(3), turned(2)
            add_rows("w_o")
            t_with_gain("g", hnT, ROW_MOE, 0)
            dve.wait_ge(squares, TC * 4)
            variance().then_inc(var_ready, 1)
            t_with_gain("g", hnT, ROW_MOE, 2)
            dve.wait_ge(root, 4)
            newton(linked)
            dve.sem_inc(rstd_ok, 1)
            bank, done = a_complete(dve, "logits")
            dve.tensor_copy(logT[:], bank[0:E, 0:SEQ]).then_inc(done, 1)
            dve.wait_ge(t_full[0], t_use("route")[1])
            dve.wait_ge(consts, N_CONSTS)
            dve.wait_ge(br_in, 16)
            for t in range(TC):
                linked(dve.scalar_tensor_tensor(out=lg[:, t, 0:E], in0=ps[:, bank_t[0], t * E:(t + 1) * E],
                                                scalar=stat[:, 3, t:t + 1], in1=br_sb[:], op0=ALU.mult, op1=ALU.add))
            for t in range(TC):
                linked(dve.max(top[:, t, :], lg[:, t, 0:E]))
            dve.tensor_scalar(small[:, 0, :], top[:, :, 0], -1.0, None, ALU.mult).then_inc(route_neg, 1)
            linked(dve.memset(top[:, :, TOP_K:8], -FAR))
            for t in range(TC):
                linked(dve.match_replace(marked[:, t, :], top[:, t, :], lg[:, t, :], FAR))
                dve.tensor_scalar(mask[:, t, :], marked[:, t, 0:E], FAR, None, ALU.is_equal).then_inc(masked, 1)
            dve.wait_ge(masked, TC)

            def gates():
                dve.wait_ge(route_exp, TC)
                for t in range(TC):
                    linked(dve.scalar_tensor_tensor(out=gate[:, t, 0:E], in0=ex[:, t, :], scalar=1.0,
                                                    in1=mask[:, t, :], op0=ALU.mult, op1=ALU.mult,
                                                    accum_out=small[:, 1, t:t + 1]))
                linked(dve.reciprocal(small[:, 2, :], small[:, 1, :]))
                for t in range(TC):
                    linked(dve.tensor_scalar(gate[:, t, 0:E], gate[:, t, 0:E], small[:, 2, t:t + 1], None, ALU.mult))

            def places():
                dve.wait_ge(ranked, 1)
                ranks = ps[:, 0, 0:TC * E].rearrange("p (c e) -> p c e", c=TC)
                linked(dve.scalar_tensor_tensor(out=place[:, :, 0:E], in0=ranks, scalar=1.0, in1=mask[:],
                                                op0=ALU.add, op1=ALU.mult))

            def counts():
                number = ps[0:1, 0, 2 * E:3 * E]
                linked(dve.tensor_copy(cnt_i[:], number))
                linked(dve.tensor_reduce(most_f[:], number, AX.X, ALU.max))
                dve.tensor_copy(most_i[:], most_f[:]).then_inc(routed, 1)

            def select(s, e, par, shift=0):
                dve.tensor_copy(onehot[par], ident[0:E, bass.ds(e, 1)].broadcast_to([E, CAP])).then_inc(onehot_ok, 1)
                at = place[:, :, bass.ds(e, 1)].broadcast_to([P, TC, CAP])
                slots = slot_no[:].unsqueeze(1).broadcast_to([P, TC, CAP])
                if shift:
                    dve.scalar_tensor_tensor(out=sel, in0=at, scalar=float(shift), in1=slots, op0=ALU.subtract,
                                             op1=ALU.is_equal).then_inc(sel_ok, 1)
                else:
                    dve.tensor_tensor(sel, slots, at, ALU.is_equal).then_inc(sel_ok, 1)

            def weigh(s, e, par):
                dve.wait_ge(sel_ok, s + 1)
                for d in range(2):
                    ins = dve.tensor_tensor(selg[par][:, :, d, :], sel,
                                            gate[:, :, bass.ds(e, 1)].broadcast_to([P, TC, CAP]), ALU.mult)
                ins.then_inc(selg_ok, 1)
                dve.wait_ge(selg_ok, s + 1)

            def tokens_out(s, par):
                dve.wait_ge(xT_full, s + 1)
                gain = vec[:, ROW_MOE:ROW_MOE + KC].rearrange("p (h j) -> p j h", h=2).unsqueeze(3).broadcast_to([P, 4, 2, CAP])
                dve.tensor_tensor(xT[par].rearrange("p (j h s) -> p j h s", j=4, h=2),
                                  ps[:, bank_t[0], :].rearrange("p (j h s) -> p j h s", j=4, h=2), gain,
                                  ALU.mult).then_inc(xT_ok, 1)

            def activate(s):
                dve.wait_ge(chunks_used, s * PER_EXPERT + (FRONT + KC))
                dve.tensor_scalar(glu, ps[:, 0, :], LIMIT, None, ALU.min).then_inc(glu_ok, 1)
                dve.tensor_scalar(lin, ps[:, 1, :], LIMIT, -LIMIT, ALU.min, ALU.max).then_inc(step_link, 1)
                dve.wait_ge(glu_ok, s + 1)
                dve.wait_ge(step_link, s * 2 + 1)
                dve.scalar_tensor_tensor(out=lin, in0=lin, scalar=1.0, in1=glu, op0=ALU.add, op1=ALU.mult).then_inc(step_link, 1)
                dve.wait_ge(step_link, s * 2 + 2)
                dve.wait_ge(sig_ok, s + 1)
                dve.tensor_tensor(act, lin, sig, ALU.mult).then_inc(act_ok, 1)

            def add_back(s):
                for t in range(TC):
                    b = 4 if t == 0 else 2
                    dve.wait_ge(sc_full, s * TC + t + 1)
                    dve.tensor_tensor(h_rows[:, t, :].rearrange("p (a n) -> p a n", a=2), ps[:, b:b + 2, :],
                                      h_rows[:, t, :].rearrange("p (a n) -> p a n", a=2), ALU.add).then_inc(sc_added, 1)
                dve.wait_ge(sc_added, s * TC + TC)

            places()
            select(0, 0, 0)
            gates()
            counts()
            weigh(0, 0, 0)
            tokens_out(0, 0)
            with dve.Fori(0, E // UNROLL) as turn:
                e0 = turn * UNROLL
                for u in range(UNROLL):
                    s = e0 + u
                    select(s + 1, s + 1, (u + 1) % 2)
                    weigh(s + 1, s + 1, (u + 1) % 2)
                    activate(s)
                    tokens_out(s + 1, (u + 1) % 2)
                    add_back(s)

            def again(b, e, k):
                s = k + E
                select(s + 1, e, 0, shift=CAP * b)
                weigh(s + 1, e, 0)
                tokens_out(s + 1, 0)
                activate(s)
                add_back(s)
            k = more_rounds(dve, again)
            ends = [0]

            def end_linked(ins):
                ends[0] += 1
                ins.then_inc(end_link, 1)
                dve.wait_ge(end_link, ends[0])
            dve.wait_ge(gfin_in, 16)
            dve.wait_ge(sc_added, k * TC + E * TC)
            for c in range(TC):
                end_linked(dve.tensor_tensor(n_rows[:, c, :], h_rows[:, c, :], gfin, ALU.mult))
            for c in range(TC):
                dve.wait_ge(end_squares, c + 1)
                variance(c).then_inc(end_var, 1)
                dve.wait_ge(end_root, c + 1)
                newton(end_linked, c)
                dve.tensor_scalar(n_rows[:, c, :], n_rows[:, c, :], stat[:, 3, c:c + 1], None,
                                  ALU.mult).then_inc(end_out, 1)


_INS = ["x", "mem", "g_mix", "w_in", "w_pool", "pool_scale", "conv_w", "w_out", "g_xattn", "g_mem", "w_q", "w_k", "w_v",
        "w_o", "g_moe", "w_router", "b_router", "w_gate_up", "b_gate_up", "w_down", "b_down", "g_final"]


def kernel(**inputs):
    import concourse.bacc as bacc
    from concourse.bass_utils import run_bass_kernel_spmd

    nc = bacc.Bacc("TRN2", target_bir_lowering=False, num_devices=1)
    arrays, args = {}, []
    for name in _INS:
        a = np.ascontiguousarray(inputs[name])
        arrays[f"in_{name}"] = a
        args.append(nc.dram_tensor(f"in_{name}", a.shape, mybir.dt.from_np(a.dtype), kind="ExternalInput").ap())
    out = nc.dram_tensor("out_h", (1, SEQ, D), F32, kind="ExternalOutput").ap()
    program(nc, *args, out)
    r = run_bass_kernel_spmd(nc, [arrays], core_ids=[0])
    return r.results[0]["out_h"]
```

```python
from contextlib import ExitStack

import numpy as np

import concourse.bass as bass
from concourse import mybir

F32 = mybir.dt.float32
F32R = mybir.dt.float32r
I32 = mybir.dt.int32
ALU = mybir.AluOpType
ACT = mybir.ActivationFunctionType
AX = mybir.AxisListType

P = 128
D = 1024
KC = D // P
SEQ = 256
TC = SEQ // P
HALF = 512
GROUPS = 4
WINDOWS = (2, 4, 8, 16)
PAD = max(WINDOWS)
CONV_K = 3
HEADS = 4
HEAD_DIM = D // HEADS
E = 32
TOP_K = 4
CAP = 64
ROUNDS = SEQ // CAP
LIMIT = 7.0
ALPHA = 1.702
EPS = 1e-5
FAR = 1e30

RING = 16
FRONT_RING = 11
CHUNK = 2048
UNROLL = 4
PER_EXPERT = 12
BODY = UNROLL * PER_EXPERT
W_IN_ORDER = (0, 1, 4, 6, 2, 5, 7, 3)
FRONT = 8 + 5 * 4
SLOT_ORDER = (6, 7, 8, 13, 9, 10, 0, 1, 14, 15, 2, 3, 12, 4, 5, 11)
HI_BUFS, LO_BUFS = 4, 2

ROW_MIX, ROW_XATTN, ROW_MEM, ROW_MOE, ROW_POOL, ROW_CONV = 0, 8, 16, 24, 32, 36
N_ROWS = 48

A_USES = ["u0", "u1", "C0", "v0", "B0", "C1", "v1", "B1", "k0", "pool0", "k1", "pool1", "k2", "k3",
          "q0", "q1", "s0", "q2", "s1", "q3", "s2", "s3", "o0", "o1", "o2", "o3", "logits"]
T_USES = [["x0", "x2", "mem0", "mem2", "h0", "h2", "P0", "P2", "g0", "g2", "route"],
          ["vec", "x1", "x3", "mem1", "mem3", "h1", "h3", "P1", "P3", "g1", "g3"]]


def a_use(name):
    return A_USES.index(name)


def t_use(name):
    b = 0 if name in T_USES[0] else 1
    return b, T_USES[b].index(name) + 1


def program(nc, x, mem, g_mix, w_in, w_pool, pool_scale, conv_w, w_out, g_xattn, g_mem, w_q, w_k,
            w_v, w_o, g_moe, w_router, b_router, w_gate_up, b_gate_up, w_down, b_down, g_final, out):
    with ExitStack() as ctx:
        def sb(name, shape, dt=F32):
            return ctx.enter_context(nc.sbuf_tensor(name, shape, dt))

        def sem(name):
            return ctx.enter_context(nc.semaphore(name))

        base = (nc.sbuf_base + 63) // 64 * 64
        sb("arena", [P, (RING + 8) * CHUNK + 1552])

        def at(name, unit, shape, dt=F32, skip=0):
            return nc.alloc_sbuf_tensor_at(name, shape, dt, offset=base + 4 * (int(unit * CHUNK) + skip))

        ring = at("ring", 0, [P, RING, CHUNK])
        mn_hi, mn_lo = at("mn_hi", 12, [P, KC, SEQ], F32R), at("mn_lo", 13, [P, KC, SEQ], F32R)
        mix_hi, mix_lo = at("mix_hi", 14, [P, KC, SEQ], F32R), at("mix_lo", 15, [P, KC, SEQ], F32R)
        mem_squares = at("mem_squares", 13, [P, TC, D])
        probsT = at("probsT", 12, [P, HEADS, TC, SEQ])
        qT = at("qT", 14, [P, KC, SEQ])
        probs = at("probs", 15, [P, TC, HEADS, SEQ])
        x_squares = at("x_squares", 17, [P, TC, D])
        h_rows = at("h_rows", 16, [P, TC, D])
        n_rows = at("n_rows", 17, [P, TC, D])
        hn_hi, hn_lo = at("hn_hi", 18, [P, KC, SEQ], F32R), at("hn_lo", 19, [P, KC, SEQ], F32R)
        gT = at("gT", 18, [P, KC, SEQ])
        mem_rows, kT = at("mem_rows", 20, [P, TC, D]), at("kT", 20, [P, KC, SEQ])
        u_pad = at("u_pad", 21, [P, GROUPS, PAD + SEQ])
        win = [at(f"win{i}", 21, [P, PAD + SEQ], skip=(GROUPS + i) * (PAD + SEQ)) for i in range(2)]
        early = at("early", 21, [P, PAD], skip=(GROUPS + 2) * (PAD + SEQ))
        v_rows = at("v_rows", 21, [P, TC, D])
        w_hi = [at(f"w_hi{i}", unit, [P, CHUNK // 2], F32R) for i, unit in enumerate((22, 22.5, 11, 11.5))]
        w_lo = [at(f"w_lo{i}", 23 + 0.5 * i, [P, CHUNK // 2], F32R) for i in range(LO_BUFS)]
        c_buf = at("c_buf", 24, [P, 2, SEQ])
        z_pad = at("z_pad", 24, [P, 2, 2 + SEQ], skip=512)
        z_acc = at("z_acc", 24, [P, SEQ], skip=1032)
        xg_sb = at("xg_sb", 19, [P, HALF])
        xT = [at(f"xT{i}", 19, [P, HALF], skip=HALF * (1 + i)) for i in range(2)]
        g_sb = at("g_sb", 19, [P, SEQ], skip=3 * HALF)
        glu, lin, sig, act = (at(n, 22, [P, HALF], skip=HALF * i) for i, n in enumerate(("glu", "lin", "sig", "act")))
        h_squares = at("h_squares", 22, [P, TC, D])
        bgu_sb = at("bgu_sb", 20, [E, 2 * D])
        actT, y_sb = at("actT", 21, [P, HALF]), at("y_sb", 21, [P, HALF], skip=HALF)
        gfin = at("gfin", 21.5, [P, D])
        bdn_sb = at("bdn_sb", 24, [E, D])
        sel = at("sel", 23, [P, TC, CAP])
        selg = [at(f"selg{i}", 23, [P, TC, 2, CAP], skip=128 + 256 * i) for i in range(2)]
        onehot = [at(f"onehot{i}", 23, [E, CAP], skip=640 + CAP * i) for i in range(2)]

        ident = sb("ident", [P, P])
        tri = sb("tri", [P, P])
        ones = sb("ones", [P, P])
        slot_no = sb("slot_no", [P, CAP])
        count_r = sb("count_r", [P, PAD])
        vec_rows = sb("vec_rows", [N_ROWS, P])
        vec = sb("vec", [P, N_ROWS])
        wp_sb = sb("wp_sb", [P, GROUPS, P])
        wr_sb = sb("wr_sb", [P, KC, E])
        br_sb = sb("br_sb", [P, E])
        stat = sb("stat", [P, 5, TC])
        warm = sb("warm", [P, 1])
        smax = sb("smax", [P, 4, HEADS, TC])
        logT = sb("logT", [E, SEQ])
        lg = sb("lg", [P, TC, E + 8])
        top = sb("top", [P, TC, 8])
        marked = sb("marked", [P, TC, E + 8])
        mask = sb("mask", [P, TC, E])
        ex = sb("ex", [P, TC, E])
        small = sb("small", [P, 3, TC])
        gate = sb("gate", [P, TC, E + 1])
        place = sb("place", [P, TC, E + 1])
        cnt_i = sb("cnt_i", [1, E], I32)
        most_f = sb("most_f", [1, 1])
        most_i = sb("most_i", [1, 1], I32)

        ps = ctx.enter_context(nc.psum_tensor("ps", [P, 8, HALF], F32))
        bank_row = (2, 3, 4, 5)
        bank_t = (6, 7)
        bank_xg, bank_y = 2, 3

        slot_full = [sem(f"slot_full{i}") for i in range(RING)]
        x_in = [sem("x_in0"), sem("x_in1")]
        mem_in, vec_in, wp_in, wr_in, br_in, bgu_in, bdn_in, gfin_in = (
            sem(n) for n in ("mem_in", "vec_in", "wp_in", "wr_in", "br_in", "bgu_in", "bdn_in", "gfin_in"))
        w_hi_ok, w_lo_ok = sem("w_hi_ok"), sem("w_lo_ok")
        halves_used = sem("halves_used")
        chunks_used = sem("chunks_used")
        hi_ok = sem("hi_ok")
        cleared, consts = sem("cleared"), sem("consts")
        a_full, a_free = sem("a_full"), [sem("a_free0"), sem("a_free1")]
        t_full, t_free = [sem("t_full0"), sem("t_full1")], [sem("t_free0"), sem("t_free1")]
        row_full, row_free = sem("row_full"), sem("row_free")
        squares, root, scaled = sem("squares"), sem("root"), sem("scaled")
        var_ready = sem("var_ready")
        mixed = sem("mixed")
        pooled = sem("pooled")
        z_used = sem("z_used")
        h_added = sem("h_added")
        neg_max, exps, probs_ok = sem("neg_max"), sem("exps"), sem("probs_ok")
        route_neg, route_exp, masked = sem("route_neg"), sem("route_exp"), sem("masked")
        rstd_ok = sem("rstd_ok")
        warmed = sem("warmed")
        ranked, routed = sem("ranked"), sem("routed")
        link = sem("link")
        step_link = sem("step_link")
        onehot_ok, sel_ok, selg_ok = sem("onehot_ok"), sem("sel_ok"), sem("selg_ok")
        xg_full, xg_ok, xT_full, xT_ok = sem("xg_full"), sem("xg_ok"), sem("xT_full"), sem("xT_ok")
        gT_full, g_ok = sem("gT_full"), sem("g_ok")
        glu_ok, sig_ok, act_ok = sem("glu_ok"), sem("sig_ok"), sem("act_ok")
        aT_full, aT_ok, y_ok = sem("aT_full"), sem("aT_ok"), sem("y_ok")
        sc_full, sc_added = sem("sc_full"), sem("sc_added")
        end_squares, end_link, stored = sem("end_squares"), sem("end_link"), sem("stored")
        end_var, end_root, end_out = sem("end_var"), sem("end_root"), sem("end_out")

        block = ctx.enter_context(nc.Block())

        def columns(w, c):
            return w[0].rearrange("(k p) n -> p k n", p=P)[:, :, 256 * c:256 * (c + 1)]

        def rows(w, c):
            return w[0, 256 * c:256 * (c + 1), :].rearrange("(a p) n -> p a n", p=P)

        front = [("w_in", columns(w_in, b)) for b in W_IN_ORDER]
        front += [("w_k", columns(w_k, c)) for c in range(4)]
        front += [("w_out", rows(w_out, c)) for c in range(4)]
        front += [("w_v", rows(w_v, c)) for c in range(4)]
        front += [("w_q", columns(w_q, c)) for c in range(4)]
        front += [("w_o", rows(w_o, c)) for c in range(4)]
        first = {name: [n for n, _ in front].index(name) for name in ("w_in", "w_k", "w_out", "w_v", "w_q", "w_o")}
        assert len(front) == FRONT and UNROLL * PER_EXPERT % RING == 0

        front_uses = [len(range(s, FRONT, FRONT_RING)) if s < FRONT_RING else 0 for s in range(RING)]

        def half_of(q, j):
            c = ring[:, q % FRONT_RING, :]
            if front[q][0] in ("w_in", "w_k", "w_q"):
                return c.rearrange("p (k n) -> p k n", k=KC)[:, :, j * P:(j + 1) * P]
            return c.rearrange("p (a n) -> p a n", a=2)[:, j:j + 1, :]

        def expert_wait(eng, n, slot, turn=None):
            have = 16 * (front_uses[slot] + n // RING + 1)
            eng.wait_ge(slot_full[slot], have if turn is None else turn * (16 * BODY // RING) + have)

        others = [n for n in A_USES if n[0] not in "uCvBkq"]
        chunk_of = {n: first["w_in"] + i for i, n in enumerate(("u0", "u1", "C0", "v0", "B0", "C1", "v1", "B1"))}
        chunk_of.update({f"{m}{h}": first[f"w_{m}"] + h for m in "kq" for h in range(4)})

        def a_complete(eng, name):
            if name in chunk_of:
                eng.wait_ge(halves_used, 2 * (chunk_of[name] + 1))
            else:
                eng.wait_ge(a_full, others.index(name) + 1)
            return ps[:, a_use(name) % 2, :], a_free[a_use(name) % 2]

        def row_complete(eng, use, r):
            if r < 3:
                eng.wait_ge(row_full, 3 * ("w_out", "w_v", "w_o").index(use) + r + 1)
            else:
                eng.wait_ge(halves_used, 2 * (first[use] + 4))

        total = E * PER_EXPERT

        def expert_source(e, c):
            if c < 8:
                return w_gate_up[0, bass.ds(e, 1), P * c:P * (c + 1), :].rearrange("o p n -> p (o n)")
            return w_down[0, bass.ds(e, 1), 256 * (c - 8):256 * (c - 7), :].rearrange("o (a p) n -> p (o a) n", p=P)

        def expert_target(slot, c):
            return ring[:, slot, :] if c < 8 else ring[:, slot, :].rearrange("p (a n) -> p a n", a=2)

        def more_rounds(eng, body):
            k_reg = eng.alloc_register(f"rounds_{eng.engine.name}")
            eng.reg_mov(k_reg, 0)
            eng.wait_ge(routed, 1)
            with eng.If(eng.value_load(most_i[0:1, 0:1], min_val=0, max_val=SEQ) > CAP):
                for b in range(1, ROUNDS):
                    with eng.Fori(0, E) as e:
                        with eng.If(eng.value_load(cnt_i[0:1, bass.ds(e, 1)], min_val=0, max_val=SEQ) > CAP * b):
                            k = eng.snap(k_reg, min_val=0, max_val=SEQ * TOP_K // CAP)
                            body(b, e, k)
                            eng.reg_add(k_reg, k_reg, 1)
            return eng.snap(k_reg, min_val=0, max_val=SEQ * TOP_K // CAP)

        @block.sync
        def _(sp):
            for c in range(TC):
                sp.dma_start(h_rows[:, c, :], x[0, P * c:P * (c + 1), :]).then_inc(x_in[c], 16)
            for q, (_, src) in enumerate(front):
                if q == 1:
                    sp.dma_start(mem_rows[:], mem[0].rearrange("(c p) d -> p c d", p=P)).then_inc(mem_in, 16)
                if q >= FRONT_RING:
                    sp.wait_ge(w_lo_ok, 2 * (q - FRONT_RING + 1))
                dst = ring[:, q % FRONT_RING, :].rearrange("p (k n) -> p k n", k=src.shape[1])
                sp.dma_start(dst, src).then_inc(slot_full[q % FRONT_RING], 16)
            for n, slot in enumerate(SLOT_ORDER):
                if slot == 13:
                    sp.wait_ge(halves_used, 2 * (first["w_v"] + 4))
                elif slot == 14:
                    a_complete(sp, "s3")
                    sp.dma_start(bgu_sb[:], b_gate_up[0]).then_inc(bgu_in, 16)
                    sp.dma_start(bdn_sb[:], b_down[0]).then_inc(bdn_in, 16)
                elif slot == 15:
                    b, uses = t_use("P3")
                    sp.wait_ge(t_full[b], uses)
                elif slot == 12:
                    a_complete(sp, "o3")
                    sp.dma_start(gfin[:], g_final.partition_broadcast(P)).then_inc(gfin_in, 16)
                elif slot == 11:
                    sp.wait_ge(halves_used, 2 * FRONT)
                else:
                    last = max(q for q in range(FRONT) if q % FRONT_RING == slot)
                    sp.wait_ge(w_lo_ok, 2 * (last + 1))
                sp.dma_start(expert_target(slot, n % PER_EXPERT), expert_source(n // PER_EXPERT, n % PER_EXPERT)) \
                    .then_inc(slot_full[slot], 16)

            def stream(n, turn=0):
                slot = SLOT_ORDER[n % RING]
                sp.wait_ge(chunks_used, turn * BODY + (n - RING + 1))
                sp.dma_start(expert_target(slot, n % PER_EXPERT),
                             expert_source(turn * UNROLL + n // PER_EXPERT, n % PER_EXPERT)).then_inc(slot_full[slot], 16)
            turns = (total - RING) // BODY
            with sp.Fori(0, turns) as turn:
                for i in range(BODY):
                    stream(RING + i, turn)
            for n in range(RING + turns * BODY, total):
                stream(n)

            def load_again(b, e, k):
                sp.wait_ge(chunks_used, k * PER_EXPERT + total)
                for c in range(PER_EXPERT):
                    slot = SLOT_ORDER[c]
                    sp.dma_start(expert_target(slot, c), expert_source(e, c)).then_inc(slot_full[slot], 16)
            more_rounds(sp, load_again)
            for c in range(TC):
                sp.wait_ge(end_out, c + 1)
                sp.dma_start(out[0, P * c:P * (c + 1), :], n_rows[:, c, :]).then_inc(stored, 16)
            sp.wait_ge(stored, 16 * TC)

        @block.gpsimd
        def _(pool):
            pool.dma_start(wp_sb[:], w_pool[0].rearrange("g c d -> c g d")).then_inc(wp_in, 16)
            pool.memset(ident[:], 0.0).then_inc(cleared, 1)
            pool.memset(tri[:], 1.0).then_inc(cleared, 1)
            pool.wait_ge(cleared, 2)
            pool.affine_select(out=ident[:], in_=ident[:], compare_op=ALU.not_equal, fill=1.0, base=0,
                               pattern=[[-1, P]], channel_multiplier=1).then_inc(consts, 1)
            pool.affine_select(out=tri[:], in_=tri[:], compare_op=ALU.is_gt, fill=0.0, base=0,
                               pattern=[[1, P]], channel_multiplier=-1).then_inc(consts, 1)
            pool.memset(ones[:], 1.0).then_inc(consts, 1)
            pool.memset(u_pad[:, :, 0:PAD], 0.0).then_inc(consts, 1)
            pool.memset(z_pad[:, :, 0:2], 0.0).then_inc(consts, 1)
            pool.iota(count_r[:], pattern=[[1, PAD]], base=1, channel_multiplier=0,
                      allow_small_or_imprecise_dtypes=True).then_inc(consts, 1)
            pool.iota(slot_no[:], pattern=[[1, CAP]], base=1, channel_multiplier=0,
                      allow_small_or_imprecise_dtypes=True).then_inc(consts, 1)
            pool.memset(gate[:, :, E:E + 1], 0.0).then_inc(consts, 1)
            pool.memset(place[:, :, E:E + 1], 0.0).then_inc(consts, 1)
            pool.memset(lg[:, :, E:E + 8], -FAR).then_inc(consts, 1)
            pool.dma_start(br_sb[:], b_router[0].partition_broadcast(P)).then_inc(br_in, 16)
            pool.dma_start(wr_sb[:], w_router[0].rearrange("(k p) e -> p k e", p=P)).then_inc(wr_in, 16)
            for j in range(2 * FRONT):
                pool.wait_ge(w_hi_ok, j + 1)
                if j >= LO_BUFS:
                    pool.wait_ge(halves_used, j - LO_BUFS + 1)
                src = half_of(j // 2, j % 2)
                shape = dict(k=src.shape[1])
                pool.tensor_tensor(w_lo[j % LO_BUFS][:].rearrange("p (k n) -> p k n", **shape), src,
                                   w_hi[j % HI_BUFS][:].rearrange("p (k n) -> p k n", **shape).bitcast(F32),
                                   ALU.subtract).then_inc(w_lo_ok, 1)
        N_CONSTS = 10

        @block.tensor
        def _(pe):
            def t_begin(name):
                b, n = t_use(name)
                if n > 1:
                    pe.wait_ge(t_free[b], n - 1)
                return ps[:, bank_t[b], :], t_full[b]

            def transpose_rows(name, src, pair):
                bank, done = t_begin(f"{name}{pair}")
                for c in range(2):
                    for t in range(TC):
                        k = 2 * pair + c
                        mm = pe.transpose(bank[:, c * SEQ + t * P:c * SEQ + (t + 1) * P],
                                          src[:, t, k * P:(k + 1) * P], ident[:])
                mm.then_inc(done, 1)

            def a_begin(name):
                n = a_use(name)
                if n >= 2:
                    pe.wait_ge(a_free[n % 2], n // 2)
                return ps[:, n % 2, :]

            def split_half(j):
                return w_hi[j % HI_BUFS], w_lo[j % LO_BUFS]

            def project_columns(name, q, src_hi, src_lo):
                bank = a_begin(name)
                for f in range(2):
                    hi, lo = (w[:].rearrange("p (k n) -> p k n", k=KC) for w in split_half(2 * q + f))
                    pe.wait_ge(w_hi_ok, 2 * q + f + 1)
                    for n, (w, src) in enumerate(((hi, src_hi), (hi, src_lo), (lo, src_hi))):
                        if n == 2:
                            pe.wait_ge(w_lo_ok, 2 * q + f + 1)
                        for k in range(KC):
                            mm = pe.matmul(bank[:, f * SEQ:(f + 1) * SEQ], w[:, k, :], src[:, k, :],
                                           start=(n == 0 and k == 0), stop=(n == 2 and k == KC - 1),
                                           skip_group_check=True)
                    mm.then_inc(halves_used, 1)

            def project_rows(use, k, src_hi, src_lo, bank_free=None):
                j = 2 * first[use] + k
                hi, lo = split_half(j)
                pe.wait_ge(w_hi_ok, j + 1)
                for n, (w, src) in enumerate(((hi, src_hi), (hi, src_lo), (lo, src_hi))):
                    if n == 2:
                        pe.wait_ge(w_lo_ok, j + 1)
                    for r in range(4):
                        t, half = r // 2, r % 2
                        if k == 0 and n == 0 and bank_free is not None:
                            pe.wait_ge(bank_free, r + 1)
                        mm = pe.matmul(ps[:, bank_row[r], :], src[:, k, t * P:(t + 1) * P],
                                       w[:, half * HALF:(half + 1) * HALF], start=(n == 0 and k == 0),
                                       stop=(n == 2 and k == KC - 1), skip_group_check=True)
                        if n == 2 and k == KC - 1 and r < 3:
                            mm.then_inc(row_full, 1)
                mm.then_inc(halves_used, 1)

            pe.wait_ge(consts, 1)
            pe.wait_ge(vec_in, 16 * 6)
            bank, done = t_begin("vec")
            pe.transpose(bank[:, 0:N_ROWS], vec_rows[:], ident[0:N_ROWS, 0:N_ROWS]).then_inc(done, 1)
            pe.wait_ge(scaled, 1)
            for pair in range(4):
                transpose_rows("x", n_rows, pair)
            for i, name in enumerate(("u0", "u1", "C0", "v0", "B0", "C1", "v1", "B1")):
                if i == 0:
                    pe.wait_ge(t_free[0], t_use("x2")[1])
                    pe.wait_ge(t_free[1], t_use("x3")[1])
                project_columns(name, first["w_in"] + i, hn_hi, hn_lo)
                if i == 1:
                    pe.wait_ge(scaled, 2)
                    for pair in range(4):
                        transpose_rows("mem", mem_rows, pair)

            def pool_product(i):
                bank = a_begin(f"pool{i}")
                pe.wait_ge(pooled, 2 * (i + 1))
                if i == 0:
                    pe.wait_ge(wp_in, 16)
                for g in range(2):
                    mm = pe.matmul(bank[:, g * SEQ:(g + 1) * SEQ], wp_sb[:, 2 * i + g, :], u_pad[:, 2 * i + g, PAD:],
                                   start=True, stop=True, skip_group_check=True)
                mm.then_inc(a_full, 1)

            pe.wait_ge(t_free[0], t_use("mem2")[1])
            pe.wait_ge(t_free[1], t_use("mem3")[1])
            for c in range(4):
                project_columns(f"k{c}", first["w_k"] + c, mn_hi, mn_lo)
                if c < 2:
                    pool_product(c)
            pe.wait_ge(mixed, 8)
            for k in range(KC):
                project_rows("w_out", k, mix_hi, mix_lo)
            for k in range(KC):
                project_rows("w_v", k, mn_hi, mn_lo, bank_free=h_added)
                if k in (4, 6):
                    pe.wait_ge(scaled, 3)
                    for pair in (k - 4, k - 3):
                        transpose_rows("h", n_rows, pair)
            pe.wait_ge(t_free[0], t_use("h2")[1])
            pe.wait_ge(t_free[1], t_use("h3")[1])

            def query(h):
                project_columns(f"q{h}", first["w_q"] + h, hn_hi, hn_lo)

            def scores(h):
                bank = a_begin(f"s{h}")
                pe.wait_ge(a_free[a_use(f"q{h}") % 2], a_use(f"q{h}") // 2 + 1)
                if h == 0:
                    pe.wait_ge(a_free[a_use("k3") % 2], a_use("k3") // 2 + 1)
                    pe.wait_ge(a_free[a_use("k2") % 2], a_use("k2") // 2 + 1)
                for t in range(TC):
                    for a in range(2):
                        mm = pe.matmul(bank[:, t * SEQ:(t + 1) * SEQ], qT[:, 2 * h + a, t * P:(t + 1) * P],
                                       kT[:, 2 * h + a, :], start=(a == 0), stop=(a == 1), skip_group_check=True)
                mm.then_inc(a_full, 1)

            def turn_probs(h):
                bank, done = t_begin(f"P{h}")
                pe.wait_ge(probs_ok, h + 1)
                for m in range(TC):
                    for t in range(TC):
                        mm = pe.transpose(bank[:, m * SEQ + t * P:m * SEQ + (t + 1) * P],
                                          probs[:, t, h, m * P:(m + 1) * P], ident[:])
                mm.then_inc(done, 1)

            def attend(h):
                bank = a_begin(f"o{h}")
                b, n = t_use(f"P{h}")
                pe.wait_ge(t_free[b], n)
                if h == 0:
                    pe.wait_ge(row_free, 4)
                for f in range(2):
                    for m in range(TC):
                        mm = pe.matmul(bank[:, f * SEQ:(f + 1) * SEQ],
                                       v_rows[:, m, (2 * h + f) * P:(2 * h + f + 1) * P], probsT[:, h, m, :],
                                       start=(m == 0), stop=(m == TC - 1), skip_group_check=True)
                mm.then_inc(a_full, 1)

            def project_head(h):
                n = a_use(f"o{h}")
                pe.wait_ge(a_free[n % 2], n // 2 + 1)
                for k in (2 * h, 2 * h + 1):
                    project_rows("w_o", k, hn_hi, hn_lo)

            query(0), query(1), scores(0)
            query(2), scores(1), turn_probs(0)
            query(3), scores(2), turn_probs(1), scores(3)
            attend(0), turn_probs(2), attend(1), turn_probs(3)
            project_head(0), attend(2)
            project_head(1), attend(3)
            project_head(2), project_head(3)
            pe.wait_ge(h_added, 8)
            for pair in range(4):
                transpose_rows("g", h_rows, pair)
            pe.wait_ge(t_free[0], t_use("g2")[1])
            pe.wait_ge(t_free[1], t_use("g3")[1])
            pe.wait_ge(wr_in, 16)
            bank = a_begin("logits")
            for k in range(KC):
                mm = pe.matmul(bank[0:E, 0:SEQ], wr_sb[:, k, :], gT[:, k, :], start=(k == 0), stop=(k == KC - 1))
            mm.then_inc(a_full, 1)
            bank, done = t_begin("route")
            n = a_use("logits")
            pe.wait_ge(a_free[n % 2], n // 2 + 1)
            for t in range(TC):
                mm = pe.transpose(bank[:, t * E:(t + 1) * E], logT[:, t * P:(t + 1) * P], ident[0:E, 0:E])
            mm.then_inc(done, 1)
            pe.wait_ge(masked, TC)
            pe.wait_ge(consts, N_CONSTS)
            bank = ps[:, 0, :]
            pe.matmul(bank[:, 0:E], tri[:], mask[:, 0, :], start=True, stop=True, skip_group_check=True)
            pe.matmul(bank[:, E:2 * E], ones[:], mask[:, 0, :], start=True, stop=False, skip_group_check=True)
            pe.matmul(bank[:, E:2 * E], tri[:], mask[:, 1, :], start=False, stop=True, skip_group_check=True)
            pe.matmul(bank[:, 2 * E:3 * E], ones[:], mask[:, 0, :], start=True, stop=False, skip_group_check=True)
            pe.matmul(bank[:, 2 * E:3 * E], ones[:], mask[:, 1, :], start=False, stop=True,
                      skip_group_check=True).then_inc(ranked, 1)

            def gather(s):
                pe.wait_ge(sel_ok, s + 1)
                for t in range(TC):
                    for half in range(2):
                        mm = pe.matmul(ps[CAP * half:CAP * (half + 1), bank_xg, :], sel[:, t, :],
                                       n_rows[:, t, half * HALF:(half + 1) * HALF], start=(t == 0), stop=(t == TC - 1),
                                       skip_group_check=True)
                mm.then_inc(xg_full, 1)

            def turn_tokens(s):
                pe.wait_ge(xg_ok, s + 1)
                for j in range(4):
                    mm = pe.transpose(ps[:, bank_t[0], j * P:(j + 1) * P], xg_sb[:, j * P:(j + 1) * P], ident[:])
                mm.then_inc(xT_full, 1)

            def gate_up(s, par, wait_chunk, ahead=1):
                pe.wait_ge(xT_ok, s + ahead)
                pe.wait_ge(onehot_ok, s + ahead)
                for bank in range(2):
                    for half in range(2):
                        pe.matmul(ps[CAP * half:CAP * (half + 1), bank, :], onehot[par][:],
                                  bgu_sb[:, bank * D + half * HALF:bank * D + (half + 1) * HALF], start=True, stop=False,
                                  skip_group_check=True)
                for k in range(KC):
                    w = wait_chunk(k)
                    lhsT = xT[par][:, (k % 4) * P + CAP * (k // 4):(k % 4) * P + CAP * (k // 4 + 1)]
                    for bank in range(2):
                        for half in range(2):
                            mm = pe.matmul(ps[CAP * half:CAP * (half + 1), bank, :], lhsT,
                                           w[:, bank * D + half * HALF:bank * D + (half + 1) * HALF], start=False,
                                           stop=(k == KC - 1), skip_group_check=True)
                    mm.then_inc(chunks_used, 1)

            def turn_gates(s, par, ahead=1):
                pe.wait_ge(selg_ok, s + ahead)
                for t in range(TC):
                    mm = pe.transpose(ps[:, bank_t[1], t * P:(t + 1) * P],
                                      selg[par][:, t, :, :].rearrange("p d s -> p (d s)"), ident[:])
                mm.then_inc(gT_full, 1)

            def turn_act(s):
                pe.wait_ge(act_ok, s + 1)
                pe.wait_ge(g_ok, s + 1)
                for j in range(4):
                    mm = pe.transpose(ps[:, bank_t[1], j * P:(j + 1) * P], act[:, j * P:(j + 1) * P], ident[:])
                mm.then_inc(aT_full, 1)

            def down(s, par, wait_chunk):
                for half in range(2):
                    pe.matmul(ps[CAP * half:CAP * (half + 1), bank_y, :], onehot[par][:],
                              bdn_sb[:, half * HALF:(half + 1) * HALF], start=True, stop=False, skip_group_check=True)
                pe.wait_ge(aT_ok, s + 1)
                for c in range(8, PER_EXPERT):
                    w = wait_chunk(c)
                    for a in range(2):
                        k = 2 * (c - 8) + a
                        lhsT = actT[:, (k % 4) * P + CAP * (k // 4):(k % 4) * P + CAP * (k // 4 + 1)]
                        for half in range(2):
                            mm = pe.matmul(ps[CAP * half:CAP * (half + 1), bank_y, :], lhsT,
                                           w[:, a * D + half * HALF:a * D + (half + 1) * HALF], start=False,
                                           stop=(k == KC - 1), skip_group_check=True)
                    mm.then_inc(chunks_used, 1)

            def scatter(s):
                pe.wait_ge(y_ok, s + 1)
                for t in range(TC):
                    for half in range(2):
                        rws = slice(CAP * half, CAP * (half + 1))
                        mm = pe.matmul(ps[:, (4 if t == 0 else 2) + half, :], g_sb[rws, t * P:(t + 1) * P],
                                       y_sb[rws, :], start=True, stop=True, skip_group_check=True)
                    mm.then_inc(sc_full, 1)

            pe.wait_ge(scaled, 3 + TC)
            gather(0)
            turn_tokens(0)
            pe.wait_ge(bgu_in, 16)
            pe.wait_ge(bdn_in, 16)
            with pe.Fori(0, E // UNROLL) as turn:
                e0 = turn * UNROLL
                for u in range(UNROLL):
                    def ring_chunk(c, u=u):
                        n = u * PER_EXPERT + c
                        expert_wait(pe, n, SLOT_ORDER[n % RING], turn)
                        return ring[:, SLOT_ORDER[n % RING], :]
                    s = e0 + u
                    gate_up(s, u % 2, ring_chunk)
                    gather(s + 1)
                    turn_gates(s, u % 2)
                    turn_tokens(s + 1)
                    turn_act(s)
                    down(s, u % 2, ring_chunk)
                    scatter(s)

            def again(b, e, k):
                s = k + E
                def ring_chunk(c):
                    slot = SLOT_ORDER[c]
                    pe.wait_ge(slot_full[slot], k * 16 + 16 * (front_uses[slot] + len(range(c, total, RING)) + 1))
                    return ring[:, slot, :]
                gather(s + 1)
                turn_tokens(s + 1)
                gate_up(s, 0, ring_chunk, ahead=2)
                turn_gates(s, 0, ahead=2)
                turn_act(s)
                down(s, 0, ring_chunk)
                scatter(s)

            more_rounds(pe, again)

        @block.scalar
        def _(act_e):
            rows_of = [(ROW_MIX, g_mix[0].rearrange("(c p) -> c p", p=P)),
                       (ROW_XATTN, g_xattn[0].rearrange("(c p) -> c p", p=P)),
                       (ROW_MEM, g_mem[0].rearrange("(c p) -> c p", p=P)),
                       (ROW_MOE, g_moe[0].rearrange("(c p) -> c p", p=P)),
                       (ROW_POOL, pool_scale[0].rearrange("(c p) -> c p", p=P)),
                       (ROW_CONV, conv_w[0].rearrange("k (c p) -> (k c) p", p=P))]
            for r, src in rows_of:
                act_e.dma_start(vec_rows[r:r + src.shape[0], :], src).then_inc(vec_in, 16)

            def copy(dst, src, done):
                act_e.activation(dst, src, ACT.Copy).then_inc(done, 1)

            def fetch_table(fn):
                fetched[0] += 1
                act_e.activation(warm[:], ones[:, 0:1], fn).then_inc(warmed, 1)
                act_e.wait_ge(warmed, fetched[0])
            fetched = [0]

            def squares_of(src, junk):
                for c in range(TC):
                    act_e.activation(junk[:, c, :], src[:, c, :], ACT.Square,
                                     accum_out=stat[:, 0, c:c + 1]).then_inc(squares, 1)

            def root_of(n):
                act_e.wait_ge(var_ready, n)
                act_e.activation(stat[:, 2, :], stat[:, 1, :], ACT.Sqrt).then_inc(root, 1)

            def t_out(name, fn):
                b, n = t_use(name)
                act_e.wait_ge(t_full[b], n)
                fn(ps[:, bank_t[b], :], t_free[b])

            def with_gain(dst, row, pair):
                def fn(bank, done):
                    for c in range(2):
                        k = 2 * pair + c
                        ins = act_e.activation(dst[:, k, :], bank[:, c * SEQ:(c + 1) * SEQ], ACT.Copy,
                                               scale=vec[:, row + k:row + k + 1])
                    ins.then_inc(done, 1)
                return fn

            def a_out(name, dst):
                bank, done = a_complete(act_e, name)
                copy(dst, bank.rearrange("p (a b) -> p a b", a=2), done)

            def hi(*halves):
                for j in halves:
                    if j % 2 == 0:
                        act_e.wait_ge(slot_full[j // 2 % FRONT_RING], 16 * (j // 2 // FRONT_RING + 1))
                    if j >= HI_BUFS:
                        act_e.wait_ge(halves_used, j - HI_BUFS + 1)
                    src = half_of(j // 2, j % 2)
                    copy(w_hi[j % HI_BUFS][:].rearrange("p (k n) -> p k n", k=src.shape[1]), src, w_hi_ok)

            def hi_tiles(name, pair, dst, row):
                t_out(f"{name}{pair}", lambda bank, done: with_gain(dst, row, pair)(bank, hi_ok))

            for c in range(TC):
                act_e.wait_ge(x_in[c], 16)
                act_e.activation(x_squares[:, c, :], h_rows[:, c, :], ACT.Square,
                                 accum_out=stat[:, 0, c:c + 1]).then_inc(squares, 1)
            root_of(1)
            t_out("vec", lambda bank, done: copy(vec[:], bank[:, 0:N_ROWS], done))
            hi(0, 1)
            act_e.wait_ge(t_free[1], 1)
            for pair in range(4):
                hi_tiles("x", pair, hn_hi, ROW_MIX)
            hi(2, 3)
            act_e.wait_ge(mem_in, 16)
            squares_of(mem_rows, mem_squares)
            root_of(2)
            hi(4)
            a_out("u0", u_pad[:, 0:2, PAD:])
            hi(5, 6)
            a_out("u1", u_pad[:, 2:4, PAD:])
            hi(7)
            for pair in range(4):
                hi_tiles("mem", pair, mn_hi, ROW_MEM)
            hi(8)
            a_out("C0", c_buf[:])
            hi(9, 10, 11, 12, 13, 14)
            act_e.wait_ge(z_used, 1)
            a_out("C1", c_buf[:])
            hi(15, 16, 17, 18, 19, 20)
            for c in range(4):
                a_out(f"k{c}", kT[:, 2 * c:2 * c + 2, :])
                hi(21 + 2 * c, 22 + 2 * c)
            hi(29, 30, 31, 32, 33, 34, 35, 36)
            act_e.wait_ge(h_added, 4)
            squares_of(h_rows, x_squares)
            root_of(3)
            hi(37, 38, 39, 40)
            hi_tiles("h", 0, hn_hi, ROW_XATTN)
            hi_tiles("h", 1, hn_hi, ROW_XATTN)
            hi(41, 42)
            hi_tiles("h", 2, hn_hi, ROW_XATTN)
            hi_tiles("h", 3, hn_hi, ROW_XATTN)
            hi(43)
            for r in range(4):
                row_complete(act_e, "w_v", r)
                copy(v_rows[:, r // 2, (r % 2) * HALF:(r % 2 + 1) * HALF], ps[:, bank_row[r], :], row_free)

            def softmax(h):
                n = a_use(f"s{h}")
                act_e.wait_ge(neg_max, h + 1)
                for t in range(TC):
                    ins = act_e.activation(probs[:, t, h, :], ps[:, n % 2, t * SEQ:(t + 1) * SEQ], ACT.Exp,
                                           bias=smax[:, 1, h, t:t + 1], scale=HEAD_DIM ** -0.5,
                                           accum_out=smax[:, 2, h, t:t + 1])
                    ins.then_inc(exps, 1)
                act_e.wait_ge(exps, TC * (h + 1))
                act_e.sem_inc(a_free[n % 2], 1)

            def out_head(h):
                bank, _ = a_complete(act_e, f"o{h}")
                copy(hn_hi[:, 2 * h:2 * h + 2, :], bank.rearrange("p (a b) -> p a b", a=2), hi_ok)

            def turned(h):
                t_out(f"P{h}", lambda bank, done: copy(probsT[:, h, :, :], bank.rearrange("p (c t) -> p c t", c=TC), done))

            def query(h):
                a_out(f"q{h}", qT[:, 2 * h:2 * h + 2, :])
            hi(44), query(0), hi(45, 46), query(1), hi(47), softmax(0)
            hi(48), query(2), hi(49), softmax(1)
            hi(50), query(3), hi(51), softmax(2), turned(1), softmax(3)
            out_head(0), out_head(1), turned(3)
            hi(52, 53), out_head(2)
            hi(54, 55), out_head(3)
            act_e.wait_ge(h_added, 8)
            squares_of(h_rows, x_squares)
            t_out("g1", with_gain(gT, ROW_MOE, 1))
            root_of(4)
            t_out("g3", with_gain(gT, ROW_MOE, 3))
            act_e.wait_ge(consts, N_CONSTS)
            fetch_table(ACT.Exp)
            act_e.wait_ge(rstd_ok, 1)
            for c in range(TC):
                act_e.activation(n_rows[:, c, :], h_rows[:, c, :], ACT.Copy, scale=stat[:, 3, c:c + 1]).then_inc(scaled, 1)
            act_e.wait_ge(route_neg, 1)
            for t in range(TC):
                act_e.activation(ex[:, t, :], lg[:, t, 0:E], ACT.Exp, bias=small[:, 0, t:t + 1]).then_inc(route_exp, 1)

            def tokens_out(s):
                act_e.wait_ge(xg_full, s + 1)
                copy(xg_sb[:], ps[:, bank_xg, :], xg_ok)

            def sigmoid(s):
                act_e.wait_ge(glu_ok, s + 1)
                act_e.activation(sig[:], glu[:], ACT.Sigmoid, scale=ALPHA).then_inc(sig_ok, 1)

            def gates_out(s):
                act_e.wait_ge(gT_full, s + 1)
                copy(g_sb[:], ps[:, bank_t[1], 0:SEQ], g_ok)

            def act_out(s):
                act_e.wait_ge(aT_full, s + 1)
                copy(actT[:], ps[:, bank_t[1], :], aT_ok)

            def y_out(s):
                act_e.wait_ge(chunks_used, s * PER_EXPERT + PER_EXPERT)
                copy(y_sb[:], ps[:, bank_y, :], y_ok)

            fetch_table(ACT.Sigmoid)
            tokens_out(0)
            with act_e.Fori(0, E) as s:
                sigmoid(s)
                tokens_out(s + 1)
                gates_out(s)
                act_out(s)
                y_out(s)

            def again(b, e, k):
                s = k + E
                tokens_out(s + 1)
                sigmoid(s)
                gates_out(s)
                act_out(s)
                y_out(s)
            k = more_rounds(act_e, again)
            fetch_table(ACT.Sqrt)
            for c in range(TC):
                act_e.wait_ge(sc_added, k * TC + (E * TC - TC + c + 1))
                act_e.activation(h_squares[:, c, :], h_rows[:, c, :], ACT.Square,
                                 accum_out=stat[:, 0, c:c + 1]).then_inc(end_squares, 1)
            for c in range(TC):
                act_e.wait_ge(end_var, c + 1)
                act_e.activation(stat[:, 2, c:c + 1], stat[:, 1, c:c + 1], ACT.Sqrt).then_inc(end_root, 1)

        @block.vector
        def _(dve):
            links = [0]

            def linked(ins):
                links[0] += 1
                ins.then_inc(link, 1)
                dve.wait_ge(link, links[0])

            def of_tokens(c):
                return slice(0, TC) if c is None else slice(c, c + 1)

            def variance(c=None):
                t = of_tokens(c)
                return dve.tensor_scalar(stat[:, 1, t], stat[:, 0, t], 1.0 / D, EPS, ALU.mult, ALU.add)

            def newton(ln, c=None):
                t = of_tokens(c)
                ln(dve.reciprocal(stat[:, 3, t], stat[:, 2, t]))
                ln(dve.tensor_tensor(stat[:, 4, t], stat[:, 3, t], stat[:, 3, t], ALU.mult))
                ln(dve.tensor_tensor(stat[:, 4, t], stat[:, 4, t], stat[:, 1, t], ALU.mult))
                ln(dve.tensor_scalar(stat[:, 4, t], stat[:, 4, t], -0.5, 1.5, ALU.mult, ALU.add))
                ln(dve.tensor_tensor(stat[:, 3, t], stat[:, 3, t], stat[:, 4, t], ALU.mult))

            def normalise(n, src, dst):
                dve.wait_ge(squares, TC * n)
                variance().then_inc(var_ready, 1)
                dve.wait_ge(root, n)
                newton(linked)
                linked(dve.tensor_scalar(dst[:, 0, :], src[:, 0, :], stat[:, 3, 0:1], None, ALU.mult))
                dve.tensor_scalar(dst[:, 1, :], src[:, 1, :], stat[:, 3, 1:2], None, ALU.mult).then_inc(scaled, 1)
                dve.wait_ge(scaled, n)

            def t_with_gain(name, dst, row, pair):
                b, n = t_use(f"{name}{pair}")
                dve.wait_ge(t_full[b], n)
                gain = vec[:, row + 2 * pair:row + 2 * pair + 2].unsqueeze(2).broadcast_to([P, 2, SEQ])
                dve.tensor_tensor(dst[:, 2 * pair:2 * pair + 2, :],
                                  ps[:, bank_t[b], :].rearrange("p (c t) -> p c t", c=2), gain,
                                  ALU.mult).then_inc(t_free[b], 1)

            def lo_tiles(n, name, pair, dst_hi, dst, row):
                b, _ = t_use(f"{name}{pair}")
                dve.wait_ge(hi_ok, n)
                for c in range(2):
                    k = 2 * pair + c
                    ins = dve.scalar_tensor_tensor(out=dst[:, k, :], in0=ps[:, bank_t[b], c * SEQ:(c + 1) * SEQ],
                                                   scalar=vec[:, row + k:row + k + 1],
                                                   in1=dst_hi[:, k, :].bitcast(F32), op0=ALU.mult, op1=ALU.subtract)
                ins.then_inc(t_free[b], 1)

            for c in range(TC):
                dve.wait_ge(x_in[c], 16)
            normalise(1, h_rows, n_rows)
            for pair in range(4):
                lo_tiles(1 + pair, "x", pair, hn_hi, hn_lo, ROW_MIX)
            normalise(2, mem_rows, mem_rows)
            dve.wait_ge(consts, N_CONSTS)
            linked(dve.reciprocal(count_r[:], count_r[:]))
            for g, w in enumerate(WINDOWS):
                if g == 2:
                    for pair in range(4):
                        lo_tiles(5 + pair, "mem", pair, mn_hi, mn_lo, ROW_MEM)
                if g % 2 == 0:
                    n = a_use(f"u{g // 2}")
                    dve.wait_ge(a_free[n % 2], n // 2 + 1)
                src, span, buf = u_pad[:, g, :], 1, 0
                while span < w:
                    lo = 2 * span - 1
                    linked(dve.tensor_tensor(win[buf][:, lo:], src[:, lo:], src[:, lo - span:PAD + SEQ - span], ALU.add))
                    src, span, buf = win[buf], 2 * span, 1 - buf
                frame = u_pad[:, g, :]
                linked(dve.tensor_tensor(early[:, 0:w], src[:, PAD:PAD + w], count_r[:, 0:w], ALU.mult))
                linked(dve.tensor_tensor(frame[:, PAD:PAD + w], early[:, 0:w], frame[:, PAD:PAD + w], ALU.subtract))
                dve.scalar_tensor_tensor(out=frame[:, PAD + w:], in0=src[:, PAD + w:], scalar=1.0 / w,
                                         in1=frame[:, PAD + w:], op0=ALU.mult, op1=ALU.subtract).then_inc(pooled, 1)
                dve.wait_ge(pooled, g + 1)
            for i in range(2):
                n = a_use(f"C{i}")
                dve.wait_ge(a_free[n % 2], n // 2 + 1)
                bank, done = a_complete(dve, f"v{i}")
                dve.tensor_tensor(z_pad[:, :, 2:], bank.rearrange("p (a t) -> p a t", a=2), c_buf[:],
                                  ALU.mult).then_inc(done, 1)
                dve.wait_ge(done, a_use(f"v{i}") // 2 + 1)
                dve.sem_inc(z_used, 1)
                bank, done = a_complete(dve, f"B{i}")
                for a in range(2):
                    def tap(k):
                        r = ROW_CONV + GROUPS * k + 2 * i + a
                        return vec[:, r:r + 1]
                    linked(dve.tensor_scalar(z_acc[:], z_pad[:, a, 2:], tap(2), None, ALU.mult))
                    for k in (1, 0):
                        linked(dve.scalar_tensor_tensor(out=z_acc[:], in0=z_pad[:, a, k:k + SEQ], scalar=tap(k),
                                                        in1=z_acc[:], op0=ALU.mult, op1=ALU.add))
                    linked(dve.tensor_tensor(z_acc[:], bank[:, a * SEQ:(a + 1) * SEQ], z_acc[:], ALU.mult))
                    linked(dve.tensor_copy(mix_hi[:, 4 + 2 * i + a, :], z_acc[:]))
                    dve.tensor_tensor(mix_lo[:, 4 + 2 * i + a, :], z_acc[:], mix_hi[:, 4 + 2 * i + a, :].bitcast(F32),
                                      ALU.subtract).then_inc(mixed, 1)
                    dve.wait_ge(mixed, 2 * i + a + 1)
                dve.sem_inc(done, 1)
            for i in range(2):
                bank, done = a_complete(dve, f"pool{i}")
                for a in range(2):
                    g = 2 * i + a
                    scale = vec[:, ROW_POOL + g:ROW_POOL + g + 1]
                    linked(dve.tensor_scalar(mix_hi[:, g, :], bank[:, a * SEQ:(a + 1) * SEQ], scale, None, ALU.mult))
                    dve.scalar_tensor_tensor(out=mix_lo[:, g, :], in0=bank[:, a * SEQ:(a + 1) * SEQ], scalar=scale,
                                             in1=mix_hi[:, g, :].bitcast(F32), op0=ALU.mult,
                                             op1=ALU.subtract).then_inc(mixed, 1)
                dve.wait_ge(mixed, 4 + 2 * i + 2)
                dve.sem_inc(done, 1)

            def add_rows(use):
                for r in range(4):
                    row_complete(dve, use, r)
                    part = h_rows[:, r // 2, (r % 2) * HALF:(r % 2 + 1) * HALF]
                    dve.tensor_tensor(part, ps[:, bank_row[r], :], part, ALU.add).then_inc(h_added, 1)
            add_rows("w_out")
            dve.wait_ge(h_added, 4)
            normalise(3, h_rows, n_rows)
            for pair in range(4):
                lo_tiles(9 + pair, "h", pair, hn_hi, hn_lo, ROW_XATTN)

            def largest(h):
                bank, _ = a_complete(dve, f"s{h}")
                linked(dve.tensor_reduce(smax[:, 0, h, :], bank.rearrange("p (c m) -> p c m", c=TC), AX.X, ALU.max))
                dve.tensor_scalar(smax[:, 1, h, :], smax[:, 0, h, :], -HEAD_DIM ** -0.5, None, ALU.mult).then_inc(neg_max, 1)

            def scale_probs(h):
                dve.wait_ge(exps, TC * (h + 1))
                linked(dve.reciprocal(smax[:, 3, h, :], smax[:, 2, h, :]))
                linked(dve.tensor_scalar(probs[:, 0, h, :], probs[:, 0, h, :], smax[:, 3, h, 0:1], None, ALU.mult))
                dve.tensor_scalar(probs[:, 1, h, :], probs[:, 1, h, :], smax[:, 3, h, 1:2], None, ALU.mult).then_inc(probs_ok, 1)

            def turned(h):
                b, n = t_use(f"P{h}")
                dve.wait_ge(t_full[b], n)
                dve.tensor_copy(probsT[:, h, :, :], ps[:, bank_t[b], :].rearrange("p (c t) -> p c t", c=TC)).then_inc(t_free[b], 1)

            def out_head(h):
                bank, done = a_complete(dve, f"o{h}")
                dve.wait_ge(hi_ok, 13 + h)
                dve.tensor_tensor(hn_lo[:, 2 * h:2 * h + 2, :], bank.rearrange("p (a b) -> p a b", a=2),
                                  hn_hi[:, 2 * h:2 * h + 2, :].bitcast(F32), ALU.subtract).then_inc(done, 1)
            largest(0), scale_probs(0), largest(1), turned(0), scale_probs(1)
            largest(2), largest(3), scale_probs(2), scale_probs(3)
            out_head(0), turned(2), out_head(1), out_head(2), out_head(3)
            add_rows("w_o")
            t_with_gain("g", gT, ROW_MOE, 0)
            dve.wait_ge(squares, TC * 4)
            variance().then_inc(var_ready, 1)
            t_with_gain("g", gT, ROW_MOE, 2)
            dve.wait_ge(root, 4)
            newton(linked)
            dve.sem_inc(rstd_ok, 1)
            bank, done = a_complete(dve, "logits")
            dve.tensor_copy(logT[:], bank[0:E, 0:SEQ]).then_inc(done, 1)
            dve.wait_ge(t_full[0], t_use("route")[1])
            dve.wait_ge(consts, N_CONSTS)
            dve.wait_ge(br_in, 16)
            for t in range(TC):
                linked(dve.scalar_tensor_tensor(out=lg[:, t, 0:E], in0=ps[:, bank_t[0], t * E:(t + 1) * E],
                                                scalar=stat[:, 3, t:t + 1], in1=br_sb[:], op0=ALU.mult, op1=ALU.add))
            for t in range(TC):
                linked(dve.max(top[:, t, :], lg[:, t, 0:E]))
            dve.tensor_scalar(small[:, 0, :], top[:, :, 0], -1.0, None, ALU.mult).then_inc(route_neg, 1)
            linked(dve.memset(top[:, :, TOP_K:8], -FAR))
            for t in range(TC):
                linked(dve.match_replace(marked[:, t, :], top[:, t, :], lg[:, t, :], FAR))
                dve.tensor_scalar(mask[:, t, :], marked[:, t, 0:E], FAR, None, ALU.is_equal).then_inc(masked, 1)
            dve.wait_ge(masked, TC)

            def gates():
                dve.wait_ge(route_exp, TC)
                for t in range(TC):
                    linked(dve.scalar_tensor_tensor(out=gate[:, t, 0:E], in0=ex[:, t, :], scalar=1.0,
                                                    in1=mask[:, t, :], op0=ALU.mult, op1=ALU.mult,
                                                    accum_out=small[:, 1, t:t + 1]))
                linked(dve.reciprocal(small[:, 2, :], small[:, 1, :]))
                for t in range(TC):
                    linked(dve.tensor_scalar(gate[:, t, 0:E], gate[:, t, 0:E], small[:, 2, t:t + 1], None, ALU.mult))

            def places():
                dve.wait_ge(ranked, 1)
                ranks = ps[:, 0, 0:TC * E].rearrange("p (c e) -> p c e", c=TC)
                linked(dve.scalar_tensor_tensor(out=place[:, :, 0:E], in0=ranks, scalar=1.0, in1=mask[:],
                                                op0=ALU.add, op1=ALU.mult))

            def counts():
                number = ps[0:1, 0, 2 * E:3 * E]
                linked(dve.tensor_copy(cnt_i[:], number))
                linked(dve.tensor_reduce(most_f[:], number, AX.X, ALU.max))
                dve.tensor_copy(most_i[:], most_f[:]).then_inc(routed, 1)

            def select(s, e, par, shift=0):
                dve.tensor_copy(onehot[par][:], ident[0:E, bass.ds(e, 1)].broadcast_to([E, CAP])).then_inc(onehot_ok, 1)
                at = place[:, :, bass.ds(e, 1)].broadcast_to([P, TC, CAP])
                slots = slot_no[:].unsqueeze(1).broadcast_to([P, TC, CAP])
                if shift:
                    dve.scalar_tensor_tensor(out=sel[:], in0=at, scalar=float(shift), in1=slots, op0=ALU.subtract,
                                             op1=ALU.is_equal).then_inc(sel_ok, 1)
                else:
                    dve.tensor_tensor(sel[:], slots, at, ALU.is_equal).then_inc(sel_ok, 1)

            def weigh(s, e, par):
                dve.wait_ge(sel_ok, s + 1)
                for d in range(2):
                    ins = dve.tensor_tensor(selg[par][:, :, d, :], sel[:],
                                            gate[:, :, bass.ds(e, 1)].broadcast_to([P, TC, CAP]), ALU.mult)
                ins.then_inc(selg_ok, 1)
                dve.wait_ge(selg_ok, s + 1)

            def tokens_out(s, par):
                dve.wait_ge(xT_full, s + 1)
                gain = vec[:, ROW_MOE:ROW_MOE + KC].rearrange("p (h j) -> p j h", h=2).unsqueeze(3).broadcast_to([P, 4, 2, CAP])
                dve.tensor_tensor(xT[par][:].rearrange("p (j h s) -> p j h s", j=4, h=2),
                                  ps[:, bank_t[0], :].rearrange("p (j h s) -> p j h s", j=4, h=2), gain,
                                  ALU.mult).then_inc(xT_ok, 1)

            def activate(s):
                dve.wait_ge(chunks_used, s * PER_EXPERT + KC)
                dve.tensor_scalar(glu[:], ps[:, 0, :], LIMIT, None, ALU.min).then_inc(glu_ok, 1)
                dve.tensor_scalar(lin[:], ps[:, 1, :], LIMIT, -LIMIT, ALU.min, ALU.max).then_inc(step_link, 1)
                dve.wait_ge(glu_ok, s + 1)
                dve.wait_ge(step_link, s * 2 + 1)
                dve.scalar_tensor_tensor(out=lin[:], in0=lin[:], scalar=1.0, in1=glu[:], op0=ALU.add, op1=ALU.mult).then_inc(step_link, 1)
                dve.wait_ge(step_link, s * 2 + 2)
                dve.wait_ge(sig_ok, s + 1)
                dve.tensor_tensor(act[:], lin[:], sig[:], ALU.mult).then_inc(act_ok, 1)

            def add_back(s):
                for t in range(TC):
                    b = 4 if t == 0 else 2
                    dve.wait_ge(sc_full, s * TC + t + 1)
                    dve.tensor_tensor(h_rows[:, t, :].rearrange("p (a n) -> p a n", a=2), ps[:, b:b + 2, :],
                                      h_rows[:, t, :].rearrange("p (a n) -> p a n", a=2), ALU.add).then_inc(sc_added, 1)
                dve.wait_ge(sc_added, s * TC + TC)

            places()
            select(0, 0, 0)
            gates()
            counts()
            weigh(0, 0, 0)
            tokens_out(0, 0)
            with dve.Fori(0, E // UNROLL) as turn:
                e0 = turn * UNROLL
                for u in range(UNROLL):
                    s = e0 + u
                    select(s + 1, s + 1, (u + 1) % 2)
                    weigh(s + 1, s + 1, (u + 1) % 2)
                    activate(s)
                    tokens_out(s + 1, (u + 1) % 2)
                    add_back(s)

            def again(b, e, k):
                s = k + E
                select(s + 1, e, 0, shift=CAP * b)
                weigh(s + 1, e, 0)
                tokens_out(s + 1, 0)
                activate(s)
                add_back(s)
            k = more_rounds(dve, again)
            ends = [0]

            def end_linked(ins):
                ends[0] += 1
                ins.then_inc(end_link, 1)
                dve.wait_ge(end_link, ends[0])
            dve.wait_ge(gfin_in, 16)
            dve.wait_ge(sc_added, k * TC + E * TC)
            for c in range(TC):
                end_linked(dve.tensor_tensor(n_rows[:, c, :], h_rows[:, c, :], gfin[:], ALU.mult))
            for c in range(TC):
                dve.wait_ge(end_squares, c + 1)
                variance(c).then_inc(end_var, 1)
                dve.wait_ge(end_root, c + 1)
                newton(end_linked, c)
                dve.tensor_scalar(n_rows[:, c, :], n_rows[:, c, :], stat[:, 3, c:c + 1], None,
                                  ALU.mult).then_inc(end_out, 1)


_INS = ["x", "mem", "g_mix", "w_in", "w_pool", "pool_scale", "conv_w", "w_out", "g_xattn", "g_mem", "w_q", "w_k", "w_v",
        "w_o", "g_moe", "w_router", "b_router", "w_gate_up", "b_gate_up", "w_down", "b_down", "g_final"]


def kernel(**inputs):
    import concourse.bacc as bacc
    from concourse.bass_utils import run_bass_kernel_spmd

    nc = bacc.Bacc("TRN2", target_bir_lowering=False, num_devices=1)
    arrays, args = {}, []
    for name in _INS:
        a = np.ascontiguousarray(inputs[name])
        arrays[f"in_{name}"] = a
        args.append(nc.dram_tensor(f"in_{name}", a.shape, mybir.dt.from_np(a.dtype), kind="ExternalInput").ap())
    out = nc.dram_tensor("out_h", (1, SEQ, D), F32, kind="ExternalOutput").ap()
    program(nc, *args, out)
    r = run_bass_kernel_spmd(nc, [arrays], core_ids=[0])
    return r.results[0]["out_h"]
```

```python
from contextlib import ExitStack

import numpy as np

import concourse.bass as bass
from concourse import mybir

F32 = mybir.dt.float32
F32R = mybir.dt.float32r
I32 = mybir.dt.int32
ALU = mybir.AluOpType
ACT = mybir.ActivationFunctionType
AX = mybir.AxisListType

P = 128
D = 1024
KC = D // P
SEQ = 256
TC = SEQ // P
HALF = 512
GROUPS = 4
WINDOWS = (2, 4, 8, 16)
PAD = max(WINDOWS)
CONV_K = 3
HEADS = 4
HEAD_DIM = D // HEADS
E = 32
TOP_K = 4
CAP = 64
ROUNDS = SEQ // CAP
LIMIT = 7.0
ALPHA = 1.702
EPS = 1e-5
FAR = 1e30

RING = 16
FRONT_RING = 10
CHUNK = 2048
UNROLL = 4
PER_EXPERT = 12
BODY = UNROLL * PER_EXPERT
W_IN_ORDER = (0, 1, 4, 6, 2, 5, 7, 3)
FRONT = 8 + 5 * 4
SLOT_ORDER = (10, 8, 9, 13, 0, 1, 2, 3, 14, 15, 4, 5, 12, 6, 7, 11)
EXTRA = 2
HI_BUFS, LO_BUFS = 4, 2

ROW_MIX, ROW_XATTN, ROW_MEM, ROW_MOE, ROW_POOL, ROW_CONV = 0, 8, 16, 24, 32, 36
N_ROWS = 48

A_USES = ["u0", "u1", "C0", "v0", "B0", "C1", "pool0", "v1", "pool1", "B1", "k0", "k1", "k2", "k3",
          "q0", "q1", "s0", "q2", "s1", "q3", "s2", "s3", "o0", "o1", "o2", "o3", "logits"]
T_USES = [["mem0", "mem2", "x0", "x2", "scale", "h0", "h2", "P0", "P2", "g0", "g2"],
          ["vec", "mem1", "mem3", "x1", "x3", "h1", "h3", "P1", "P3", "g1", "g3"]]
HI_ORDER = [f"{name}{i}" for name in ("mem", "x", "h", "o") for i in range(4)]


def a_use(name):
    return A_USES.index(name)


def t_use(name):
    b = 0 if name in T_USES[0] else 1
    return b, T_USES[b].index(name) + 1


def program(nc, x, mem, g_mix, w_in, w_pool, pool_scale, conv_w, w_out, g_xattn, g_mem, w_q, w_k,
            w_v, w_o, g_moe, w_router, b_router, w_gate_up, b_gate_up, w_down, b_down, g_final, out):
    with ExitStack() as ctx:
        def sb(name, shape, dt=F32):
            return ctx.enter_context(nc.sbuf_tensor(name, shape, dt))

        def sem(name):
            return ctx.enter_context(nc.semaphore(name))

        base = (nc.sbuf_base + 63) // 64 * 64
        sb("arena", [P, (RING + 8) * CHUNK + 1552])

        def at(name, unit, shape, dt=F32, skip=0):
            return nc.alloc_sbuf_tensor_at(name, shape, dt, offset=base + 4 * (int(unit * CHUNK) + skip))

        ring = at("ring", 0, [P, RING, CHUNK])
        mn_hi, mn_lo = at("mn_hi", 12, [P, KC, SEQ], F32R), at("mn_lo", 13, [P, KC, SEQ], F32R)
        mix_hi, mix_lo = at("mix_hi", 14, [P, KC, SEQ], F32R), at("mix_lo", 15, [P, KC, SEQ], F32R)
        mem_squares = at("mem_squares", 14, [P, TC, D])
        probsT = at("probsT", 12, [P, HEADS, TC, SEQ])
        qT = at("qT", 14, [P, KC, SEQ])
        probs = at("probs", 15, [P, TC, HEADS, SEQ])
        x_squares = at("x_squares", 17, [P, TC, D])
        h_rows = at("h_rows", 16, [P, TC, D])
        n_rows = at("n_rows", 17, [P, TC, D])
        hn_hi, hn_lo = at("hn_hi", 18, [P, KC, SEQ], F32R), at("hn_lo", 19, [P, KC, SEQ], F32R)
        gT = at("gT", 18, [P, KC, SEQ])
        mem_rows, kT = at("mem_rows", 20, [P, TC, D]), at("kT", 20, [P, KC, SEQ])
        u_pad = at("u_pad", 10, [P, GROUPS, PAD + SEQ])
        win = [at(f"win{i}", 10, [P, PAD + SEQ], skip=(GROUPS + i) * (PAD + SEQ)) for i in range(2)]
        early = at("early", 10, [P, PAD], skip=(GROUPS + 2) * (PAD + SEQ))
        v_rows = at("v_rows", 21, [P, TC, D])
        w_hi = [at(f"w_hi{i}", unit, [P, CHUNK // 2], F32R) for i, unit in enumerate((22, 22.5, 11, 11.5))]
        w_lo = [at(f"w_lo{i}", 23 + 0.5 * i, [P, CHUNK // 2], F32R) for i in range(LO_BUFS)]
        c_buf = at("c_buf", 24, [P, 2, SEQ])
        z_pad = at("z_pad", 24, [P, 2, 2 + SEQ], skip=512)
        z_acc = at("z_acc", 24, [P, SEQ], skip=1032)
        mem_scale = at("mem_scale", 24, [P, SEQ], skip=1032 + SEQ)
        xg_sb = at("xg_sb", 19, [P, HALF])
        xT = [at(f"xT{i}", 19, [P, HALF], skip=HALF * (1 + i)) for i in range(2)]
        g_sb = at("g_sb", 19, [P, SEQ], skip=3 * HALF)
        glu, lin, sig, act = (at(n, 22, [P, HALF], skip=HALF * i) for i, n in enumerate(("glu", "lin", "sig", "act")))
        h_squares = at("h_squares", 22, [P, TC, D])
        bgu_sb = at("bgu_sb", 20, [E, 2 * D])
        actT, y_sb = at("actT", 21, [P, HALF]), at("y_sb", 21, [P, HALF], skip=HALF)
        extra = [at("extra0", 23, [P, CHUNK]), at("extra1", 18, [P, CHUNK])]
        gfin = at("gfin", 18, [P, D])
        bdn_sb = at("bdn_sb", 24, [E, D])
        sel = at("sel", 21.5, [P, TC, CAP])
        selg = [at(f"selg{i}", 21.5, [P, TC, 2, CAP], skip=128 + 256 * i) for i in range(2)]
        onehot = [at(f"onehot{i}", 21.5, [E, CAP], skip=640 + CAP * i) for i in range(2)]

        ident = sb("ident", [P, P])
        tri = sb("tri", [P, P])
        ones = sb("ones", [P, P])
        slot_no = sb("slot_no", [P, CAP])
        count_r = sb("count_r", [P, PAD])
        vec_rows = sb("vec_rows", [N_ROWS, P])
        vec = sb("vec", [P, N_ROWS])
        wp_sb = sb("wp_sb", [P, GROUPS, P])
        wr_sb = sb("wr_sb", [P, KC, E])
        br_sb = sb("br_sb", [P, E])
        stat = sb("stat", [P, 5, 4, TC])
        eps = sb("eps", [P, 1])
        warm = sb("warm", [P, 1])
        smax = sb("smax", [P, 4, HEADS, TC])
        lg = sb("lg", [P, TC, E + 8])
        top = sb("top", [P, TC, 8])
        marked = sb("marked", [P, TC, E + 8])
        mask = sb("mask", [P, TC, E])
        ex = sb("ex", [P, TC, E])
        small = sb("small", [P, 3, TC])
        gate = sb("gate", [P, TC, E + 1])
        place = sb("place", [P, TC, E + 1])
        cnt_i = sb("cnt_i", [1, E], I32)
        most_f = sb("most_f", [1, 1])
        most_i = sb("most_i", [1, 1], I32)

        ps = ctx.enter_context(nc.psum_tensor("ps", [P, 8, HALF], F32))
        bank_row = (2, 3, 4, 5)
        bank_t = (6, 7)
        bank_xg, bank_y = 2, 3

        slot_full = [sem(f"slot_full{i}") for i in range(RING)]
        extra_full = [sem(f"extra_full{i}") for i in range(EXTRA)]
        x_in = [sem("x_in0"), sem("x_in1")]
        mem_in = [sem("mem_in0"), sem("mem_in1")]
        vec_in, wp_in, wr_in, br_in, bgu_in, bdn_in, gfin_in = (
            sem(n) for n in ("vec_in", "wp_in", "wr_in", "br_in", "bgu_in", "bdn_in", "gfin_in"))
        w_hi_ok, w_lo_ok = sem("w_hi_ok"), sem("w_lo_ok")
        halves_used = sem("halves_used")
        chunks_used = sem("chunks_used")
        mem_rstd_ok, diag_ok = sem("mem_rstd_ok"), sem("diag_ok")
        hi_ok = sem("hi_ok")
        cleared, consts = sem("cleared"), sem("consts")
        a_full, a_free = sem("a_full"), [sem("a_free0"), sem("a_free1")]
        t_full, t_free = [sem("t_full0"), sem("t_full1")], [sem("t_free0"), sem("t_free1")]
        row_full, row_free = sem("row_full"), sem("row_free")
        squares, root, scaled = sem("squares"), sem("root"), sem("scaled")
        mixed = sem("mixed")
        pooled = sem("pooled")
        z_used = sem("z_used")
        h_added = sem("h_added")
        neg_max, exps, probs_ok = sem("neg_max"), sem("exps"), sem("probs_ok")
        route_neg, route_exp, masked = sem("route_neg"), sem("route_exp"), sem("masked")
        rstd_ok = sem("rstd_ok")
        warmed = sem("warmed")
        ranked, counted, routed = sem("ranked"), sem("counted"), sem("routed")
        link = sem("link")
        step_link = sem("step_link")
        onehot_ok, sel_ok, selg_ok = sem("onehot_ok"), sem("sel_ok"), sem("selg_ok")
        xg_full, xg_ok, xT_full, xT_ok = sem("xg_full"), sem("xg_ok"), sem("xT_full"), sem("xT_ok")
        gT_full, g_ok = sem("gT_full"), sem("g_ok")
        glu_ok, sig_ok, act_ok = sem("glu_ok"), sem("sig_ok"), sem("act_ok")
        aT_full, aT_ok, y_ok = sem("aT_full"), sem("aT_ok"), sem("y_ok")
        sc_full, sc_added = sem("sc_full"), sem("sc_added")
        end_squares, end_link, stored = sem("end_squares"), sem("end_link"), sem("stored")
        end_root, end_out = sem("end_root"), sem("end_out")

        block = ctx.enter_context(nc.Block())

        def columns(w, c):
            return w[0].rearrange("(k p) n -> p k n", p=P)[:, :, 256 * c:256 * (c + 1)]

        def rows(w, c):
            return w[0, 256 * c:256 * (c + 1), :].rearrange("(a p) n -> p a n", p=P)

        front = [("w_v", rows(w_v, c)) for c in range(4)]
        front += [("w_in", columns(w_in, b)) for b in W_IN_ORDER]
        front += [("w_k", columns(w_k, 0))]
        front += [("w_out", rows(w_out, c)) for c in range(4)]
        front += [("w_k", columns(w_k, c)) for c in range(1, 4)]
        front += [("w_q", columns(w_q, c)) for c in range(4)]
        front += [("w_o", rows(w_o, c)) for c in range(4)]
        first = {name: [n for n, _ in front].index(name) for name in ("w_in", "w_k", "w_out", "w_v", "w_q", "w_o")}
        assert len(front) == FRONT and UNROLL * PER_EXPERT % RING == 0

        front_uses = [len(range(s, FRONT, FRONT_RING)) if s < FRONT_RING else 0 for s in range(RING)]

        def half_of(q, j):
            c = ring[:, q % FRONT_RING, :]
            if front[q][0] in ("w_in", "w_k", "w_q"):
                return c.rearrange("p (k n) -> p k n", k=KC)[:, :, j * P:(j + 1) * P]
            return c.rearrange("p (a n) -> p a n", a=2)[:, j:j + 1, :]

        def ring_place(n):
            return n if n < RING else n - EXTRA

        def expert_chunk(eng, n, turn=None):
            if turn is None and RING <= n < RING + EXTRA:
                eng.wait_ge(extra_full[n - RING], 16)
                return extra[n - RING][:]
            m = ring_place(n) if turn is None else n - EXTRA
            slot = SLOT_ORDER[m % RING]
            have = 16 * (front_uses[slot] + m // RING + 1)
            eng.wait_ge(slot_full[slot], have if turn is None else turn * (16 * BODY // RING) + have)
            return ring[:, slot, :]

        others = [n for n in A_USES if n[0] not in "uCvBkq"]
        chunk_of = {n: first["w_in"] + i for i, n in enumerate(("u0", "u1", "C0", "v0", "B0", "C1", "v1", "B1"))}
        for m in "kq":
            chunk_of.update({f"{m}{h}": q for h, q in enumerate(q for q in range(FRONT) if front[q][0] == f"w_{m}")})

        def a_complete(eng, name):
            if name in chunk_of:
                eng.wait_ge(halves_used, 2 * (chunk_of[name] + 1))
            else:
                eng.wait_ge(a_full, others.index(name) + 1)
            return ps[:, a_use(name) % 2, :], a_free[a_use(name) % 2]

        def row_complete(eng, use, r):
            if r < 3:
                eng.wait_ge(row_full, 3 * ("w_v", "w_out", "w_o").index(use) + r + 1)
            else:
                eng.wait_ge(halves_used, 2 * (first[use] + 4))

        total = E * PER_EXPERT

        def expert_source(e, c):
            if c < 8:
                return w_gate_up[0, bass.ds(e, 1), P * c:P * (c + 1), :].rearrange("o p n -> p (o n)")
            return w_down[0, bass.ds(e, 1), 256 * (c - 8):256 * (c - 7), :].rearrange("o (a p) n -> p (o a) n", p=P)

        def as_target(buffer, c):
            return buffer if c < 8 else buffer.rearrange("p (a n) -> p a n", a=2)

        def load_most(eng):
            eng.wait_ge(routed, 1)
            return eng.value_load(most_i[0:1, 0:1], min_val=0, max_val=SEQ)

        def more_rounds(eng, most, body):
            k_reg = eng.alloc_register(f"rounds_{eng.engine.name}")
            eng.reg_mov(k_reg, 0)
            with eng.If(most > CAP):
                for b in range(1, ROUNDS):
                    with eng.Fori(0, E) as e:
                        with eng.If(eng.value_load(cnt_i[0:1, bass.ds(e, 1)], min_val=0, max_val=SEQ) > CAP * b):
                            k = eng.snap(k_reg, min_val=0, max_val=SEQ * TOP_K // CAP)
                            body(b, e, k)
                            eng.reg_add(k_reg, k_reg, 1)
            return eng.snap(k_reg, min_val=0, max_val=SEQ * TOP_K // CAP)

        @block.sync
        def _(sp):
            for c in range(TC):
                sp.dma_start(mem_rows[:, c, :], mem[0, P * c:P * (c + 1), :]).then_inc(mem_in[c], 16)
            rows_of = [(ROW_MIX, g_mix[0].rearrange("(c p) -> c p", p=P)),
                       (ROW_XATTN, g_xattn[0].rearrange("(c p) -> c p", p=P)),
                       (ROW_MEM, g_mem[0].rearrange("(c p) -> c p", p=P)),
                       (ROW_MOE, g_moe[0].rearrange("(c p) -> c p", p=P)),
                       (ROW_POOL, pool_scale[0].rearrange("(c p) -> c p", p=P)),
                       (ROW_CONV, conv_w[0].rearrange("k (c p) -> (k c) p", p=P))]
            for r, src in rows_of:
                sp.dma_start(vec_rows[r:r + src.shape[0], :], src).then_inc(vec_in, 16)
            for q, (_, src) in enumerate(front):
                if q == 2:
                    for c in range(TC):
                        sp.dma_start(h_rows[:, c, :], x[0, P * c:P * (c + 1), :]).then_inc(x_in[c], 16)
                if q >= FRONT_RING:
                    sp.wait_ge(w_lo_ok, 2 * (q - FRONT_RING + 1))
                dst = ring[:, q % FRONT_RING, :].rearrange("p (k n) -> p k n", k=src.shape[1])
                sp.dma_start(dst, src).then_inc(slot_full[q % FRONT_RING], 16)
            for n, slot in enumerate(SLOT_ORDER):
                if slot == 10:
                    sp.wait_ge(mixed, 8)
                elif slot == 13:
                    a_complete(sp, "k3")
                elif slot == 14:
                    a_complete(sp, "s3")
                    sp.dma_start(bgu_sb[:], b_gate_up[0]).then_inc(bgu_in, 16)
                    sp.dma_start(bdn_sb[:], b_down[0]).then_inc(bdn_in, 16)
                elif slot == 15:
                    b, uses = t_use("P3")
                    sp.wait_ge(t_full[b], uses)
                elif slot == 12:
                    a_complete(sp, "o3")
                elif slot == 11:
                    sp.wait_ge(halves_used, 2 * FRONT)
                else:
                    last = max(q for q in range(FRONT) if q % FRONT_RING == slot)
                    sp.wait_ge(w_lo_ok, 2 * (last + 1))
                sp.dma_start(as_target(ring[:, slot, :], n % PER_EXPERT),
                             expert_source(n // PER_EXPERT, n % PER_EXPERT)).then_inc(slot_full[slot], 16)

            for i in range(EXTRA):
                if i == 0:
                    sp.wait_ge(halves_used, 2 * FRONT)
                else:
                    a_complete(sp, "logits")
                n = RING + i
                sp.dma_start(as_target(extra[i][:], n % PER_EXPERT),
                             expert_source(n // PER_EXPERT, n % PER_EXPERT)).then_inc(extra_full[i], 16)

            def stream(n, turn=0):
                slot = SLOT_ORDER[(n - EXTRA) % RING]
                before = n - RING if n >= 2 * RING + EXTRA else n - RING - EXTRA
                sp.wait_ge(chunks_used, turn * BODY + (before + 1))
                sp.dma_start(as_target(ring[:, slot, :], n % PER_EXPERT),
                             expert_source(turn * UNROLL + n // PER_EXPERT, n % PER_EXPERT)).then_inc(slot_full[slot], 16)
            most = load_most(sp)
            for n in range(RING + EXTRA, 2 * RING + EXTRA):
                stream(n)
            streamed = 2 * RING + EXTRA
            turns = (total - streamed) // BODY
            with sp.Fori(0, turns) as turn:
                for i in range(BODY):
                    stream(streamed + i, turn)
            sp.dma_start(gfin[:], g_final.partition_broadcast(P)).then_inc(gfin_in, 16)
            for n in range(streamed + turns * BODY, total):
                stream(n)

            def load_again(b, e, k):
                sp.wait_ge(chunks_used, k * PER_EXPERT + total)
                for c in range(PER_EXPERT):
                    slot = SLOT_ORDER[c]
                    sp.dma_start(as_target(ring[:, slot, :], c), expert_source(e, c)).then_inc(slot_full[slot], 16)
            more_rounds(sp, most, load_again)
            for c in range(TC):
                for half in range(2):
                    part = slice(half * HALF, (half + 1) * HALF)
                    sp.wait_ge(end_out, 2 * c + half + 1)
                    sp.dma_start(out[0, P * c:P * (c + 1), part], n_rows[:, c, part]).then_inc(stored, 16)
            sp.wait_ge(stored, 16 * TC * 2)

        @block.gpsimd
        def _(pool):
            pool.memset(ident[:], 0.0).then_inc(cleared, 1)
            pool.memset(tri[:], 1.0).then_inc(cleared, 1)
            pool.wait_ge(cleared, 2)
            pool.affine_select(out=ident[:], in_=ident[:], compare_op=ALU.not_equal, fill=1.0, base=0,
                               pattern=[[-1, P]], channel_multiplier=1).then_inc(consts, 1)
            pool.affine_select(out=tri[:], in_=tri[:], compare_op=ALU.is_gt, fill=0.0, base=0,
                               pattern=[[1, P]], channel_multiplier=-1).then_inc(consts, 1)
            pool.memset(ones[:], 1.0).then_inc(consts, 1)
            pool.memset(eps[:], EPS).then_inc(consts, 1)
            pool.memset(u_pad[:, :, 0:PAD], 0.0).then_inc(consts, 1)
            pool.memset(z_pad[:, :, 0:2], 0.0).then_inc(consts, 1)
            pool.iota(count_r[:], pattern=[[1, PAD]], base=1, channel_multiplier=0,
                      allow_small_or_imprecise_dtypes=True).then_inc(consts, 1)
            pool.iota(slot_no[:], pattern=[[1, CAP]], base=1, channel_multiplier=0,
                      allow_small_or_imprecise_dtypes=True).then_inc(consts, 1)
            pool.memset(gate[:, :, E:E + 1], 0.0).then_inc(consts, 1)
            pool.memset(place[:, :, E:E + 1], 0.0).then_inc(consts, 1)
            pool.memset(lg[:, :, E:E + 8], -FAR).then_inc(consts, 1)
            pool.dma_start(wp_sb[:], w_pool[0].rearrange("g c d -> c g d")).then_inc(wp_in, 16)
            pool.dma_start(br_sb[:], b_router[0].partition_broadcast(P)).then_inc(br_in, 16)
            pool.dma_start(wr_sb[:], w_router[0].rearrange("(k p) e -> p k e", p=P)).then_inc(wr_in, 16)
            for j in range(2 * FRONT):
                pool.wait_ge(w_hi_ok, j + 1)
                if j >= LO_BUFS:
                    pool.wait_ge(halves_used, j - LO_BUFS + 1)
                src = half_of(j // 2, j % 2)
                shape = dict(k=src.shape[1])
                pool.tensor_tensor(w_lo[j % LO_BUFS][:].rearrange("p (k n) -> p k n", **shape), src,
                                   w_hi[j % HI_BUFS][:].rearrange("p (k n) -> p k n", **shape).bitcast(F32),
                                   ALU.subtract).then_inc(w_lo_ok, 1)
        N_CONSTS = 11

        @block.tensor
        def _(pe):
            def t_begin(name):
                b, n = t_use(name)
                if n > 1:
                    pe.wait_ge(t_free[b], n - 1)
                return ps[:, bank_t[b], :], t_full[b]

            def transpose_rows(name, src, pair):
                bank, done = t_begin(f"{name}{pair}")
                for c in range(2):
                    for t in range(TC):
                        k = 2 * pair + c
                        mm = pe.transpose(bank[:, c * SEQ + t * P:c * SEQ + (t + 1) * P],
                                          src[:, t, k * P:(k + 1) * P], ident[:])
                mm.then_inc(done, 1)

            def keep_clock(n):
                for _ in range(n):
                    pe.matmul(ps[:, bank_row[3], 0:P], ident[:], ident[:], start=True, stop=True)

            def a_begin(name):
                n = a_use(name)
                if n >= 2:
                    pe.wait_ge(a_free[n % 2], n // 2)
                return ps[:, n % 2, :]

            def split_half(j):
                return w_hi[j % HI_BUFS], w_lo[j % LO_BUFS]

            def column_half(bank, j, src_hi, src_lo):
                hi, lo = (w[:].rearrange("p (k n) -> p k n", k=KC) for w in split_half(j))
                pe.wait_ge(w_hi_ok, j + 1)
                for n, (w, src) in enumerate(((hi, src_hi), (hi, src_lo), (lo, src_hi))):
                    if n == 2:
                        pe.wait_ge(w_lo_ok, j + 1)
                    for k in range(KC):
                        mm = pe.matmul(bank[:, (j % 2) * SEQ:(j % 2 + 1) * SEQ], w[:, k, :], src[:, k, :],
                                       start=(n == 0 and k == 0), stop=(n == 2 and k == KC - 1),
                                       skip_group_check=True)
                mm.then_inc(halves_used, 1)

            def project_columns(name, src_hi, src_lo):
                bank = a_begin(name)
                for f in range(2):
                    column_half(bank, 2 * chunk_of[name] + f, src_hi, src_lo)

            def project_rows(use, k, src_hi, src_lo, bank_free=None):
                j = 2 * first[use] + k
                hi, lo = split_half(j)
                pe.wait_ge(w_hi_ok, j + 1)
                passes = ((hi, src_hi), (hi, src_lo), (lo, src_hi))
                order = [(n, r) for n in range(3) for r in range(4)]
                if k == KC - 1:
                    order.sort(key=lambda step: step[1])
                for n, r in order:
                    if (n, r) == (2, 0):
                        pe.wait_ge(w_lo_ok, j + 1)
                    if k == 0 and n == 0 and bank_free is not None:
                        pe.wait_ge(bank_free, r + 1)
                    t, half = r % 2, r // 2
                    w, src = passes[n]
                    mm = pe.matmul(ps[:, bank_row[r], :], src[:, k, t * P:(t + 1) * P],
                                   w[:, half * HALF:(half + 1) * HALF], start=(n == 0 and k == 0),
                                   stop=(n == 2 and k == KC - 1), skip_group_check=True)
                    if n == 2 and k == KC - 1 and r < 3:
                        mm.then_inc(row_full, 1)
                mm.then_inc(halves_used, 1)

            pe.wait_ge(consts, 1)
            keep_clock(9)
            pe.wait_ge(vec_in, 16 * 6)
            bank, done = t_begin("vec")
            pe.transpose(bank[:, 0:N_ROWS], vec_rows[:], ident[0:N_ROWS, 0:N_ROWS]).then_inc(done, 1)
            for c in range(TC):
                pe.wait_ge(mem_in[c], 16)
            for pair in range(4):
                transpose_rows("mem", mem_rows, pair)
            for k in range(KC):
                b, n = t_use(f"mem{k // 2}")
                pe.wait_ge(t_free[b], n)
                project_rows("w_v", k, mn_hi, mn_lo)
                if k in (4, 6):
                    pe.wait_ge(scaled, 1)
                    for pair in (k - 4, k - 3):
                        transpose_rows("x", n_rows, pair)

            def pool_product(i):
                bank = a_begin(f"pool{i}")
                pe.wait_ge(pooled, 2 * (i + 1))
                if i == 0:
                    pe.wait_ge(wp_in, 16)
                for g in range(2):
                    mm = pe.matmul(bank[:, g * SEQ:(g + 1) * SEQ], wp_sb[:, 2 * i + g, :], u_pad[:, 2 * i + g, PAD:],
                                   start=True, stop=True, skip_group_check=True)
                mm.then_inc(a_full, 1)

            pe.wait_ge(t_free[0], t_use("x2")[1])
            pe.wait_ge(t_free[1], t_use("x3")[1])
            for name in A_USES[:A_USES.index("k0")]:
                if name.startswith("pool"):
                    pool_product(int(name[-1]))
                else:
                    project_columns(name, hn_hi, hn_lo)
                if name == "u1":
                    bank, done = t_begin("scale")
                    pe.wait_ge(diag_ok, 1)
                    pe.wait_ge(consts, N_CONSTS)
                    pe.matmul(bank[:, 0:SEQ], ones[:], z_acc[:], start=True, stop=True).then_inc(done, 1)
            project_columns("k0", mn_hi, mn_lo)
            pe.wait_ge(mixed, 8)
            for k in range(KC):
                project_rows("w_out", k, mix_hi, mix_lo, bank_free=row_free)
            project_columns("k1", mn_hi, mn_lo)
            project_columns("k2", mn_hi, mn_lo)
            pe.wait_ge(scaled, 2)
            transpose_rows("h", n_rows, 0), transpose_rows("h", n_rows, 1)
            bank = a_begin("k3")
            column_half(bank, 2 * chunk_of["k3"], mn_hi, mn_lo)
            transpose_rows("h", n_rows, 2), transpose_rows("h", n_rows, 3)
            column_half(bank, 2 * chunk_of["k3"] + 1, mn_hi, mn_lo)
            pe.wait_ge(t_free[0], t_use("h2")[1])
            pe.wait_ge(t_free[1], t_use("h3")[1])

            def query(h):
                project_columns(f"q{h}", hn_hi, hn_lo)

            def scores(h):
                bank = a_begin(f"s{h}")
                pe.wait_ge(a_free[a_use(f"q{h}") % 2], a_use(f"q{h}") // 2 + 1)
                if h == 0:
                    pe.wait_ge(a_free[a_use("k3") % 2], a_use("k3") // 2 + 1)
                    pe.wait_ge(a_free[a_use("k2") % 2], a_use("k2") // 2 + 1)
                for t in range(TC):
                    for a in range(2):
                        mm = pe.matmul(bank[:, t * SEQ:(t + 1) * SEQ], qT[:, 2 * h + a, t * P:(t + 1) * P],
                                       kT[:, 2 * h + a, :], start=(a == 0), stop=(a == 1), skip_group_check=True)
                mm.then_inc(a_full, 1)

            def turn_probs(h):
                bank, done = t_begin(f"P{h}")
                pe.wait_ge(probs_ok, h + 1)
                for m in range(TC):
                    for t in range(TC):
                        mm = pe.transpose(bank[:, m * SEQ + t * P:m * SEQ + (t + 1) * P],
                                          probs[:, t, h, m * P:(m + 1) * P], ident[:])
                mm.then_inc(done, 1)

            def attend(h):
                bank = a_begin(f"o{h}")
                b, n = t_use(f"P{h}")
                pe.wait_ge(t_free[b], n)
                if h == 0:
                    pe.wait_ge(row_free, 4)
                for f in range(2):
                    for m in range(TC):
                        mm = pe.matmul(bank[:, f * SEQ:(f + 1) * SEQ],
                                       v_rows[:, m, (2 * h + f) * P:(2 * h + f + 1) * P], probsT[:, h, m, :],
                                       start=(m == 0), stop=(m == TC - 1), skip_group_check=True)
                mm.then_inc(a_full, 1)

            def project_head(h):
                n = a_use(f"o{h}")
                pe.wait_ge(a_free[n % 2], n // 2 + 1)
                for k in (2 * h, 2 * h + 1):
                    project_rows("w_o", k, hn_hi, hn_lo, bank_free=h_added)

            query(0), query(1), scores(0)
            query(2), scores(1), turn_probs(0)
            query(3), scores(2), turn_probs(1), scores(3)
            attend(0), turn_probs(2), attend(1), turn_probs(3)
            project_head(0), attend(2)
            project_head(1), attend(3)
            project_head(2), project_head(3)
            a_begin("logits")
            pe.wait_ge(wr_in, 16)

            def logits(pair):
                b, n = t_use(f"g{pair}")
                pe.wait_ge(t_free[b], n)
                for k in (2 * pair, 2 * pair + 1):
                    for t in range(TC):
                        mm = pe.matmul(ps[:, t, 0:E], gT[:, k, t * P:(t + 1) * P], wr_sb[:, k, :],
                                       start=(k == 0), stop=(k == KC - 1), skip_group_check=True)
                return mm
            pe.wait_ge(h_added, 6)
            transpose_rows("g", h_rows, 0), transpose_rows("g", h_rows, 1)
            pe.wait_ge(h_added, 8)
            transpose_rows("g", h_rows, 2), logits(0)
            transpose_rows("g", h_rows, 3), logits(1)
            logits(2), logits(3).then_inc(a_full, 1)
            keep_clock(8)
            pe.wait_ge(masked, TC)
            pe.wait_ge(consts, N_CONSTS)
            bank = ps[:, 0, :]
            pe.matmul(bank[:, 0:E], tri[:], mask[:, 0, :], start=True, stop=True, skip_group_check=True)
            pe.matmul(bank[:, E:2 * E], ones[:], mask[:, 0, :], start=True, stop=False, skip_group_check=True)
            pe.matmul(bank[:, E:2 * E], tri[:], mask[:, 1, :], start=False, stop=True,
                      skip_group_check=True).then_inc(ranked, 1)
            pe.matmul(ps[:, 1, 0:E], ones[:], mask[:, 0, :], start=True, stop=False, skip_group_check=True)
            pe.matmul(ps[:, 1, 0:E], ones[:], mask[:, 1, :], start=False, stop=True,
                      skip_group_check=True).then_inc(counted, 1)

            def gather(s):
                pe.wait_ge(sel_ok, s + 1)
                for t in range(TC):
                    for half in range(2):
                        mm = pe.matmul(ps[CAP * half:CAP * (half + 1), bank_xg, :], sel[:, t, :],
                                       n_rows[:, t, half * HALF:(half + 1) * HALF], start=(t == 0), stop=(t == TC - 1),
                                       skip_group_check=True)
                mm.then_inc(xg_full, 1)

            def turn_tokens(s):
                pe.wait_ge(xg_ok, s + 1)
                for j in range(4):
                    mm = pe.transpose(ps[:, bank_t[0], j * P:(j + 1) * P], xg_sb[:, j * P:(j + 1) * P], ident[:])
                mm.then_inc(xT_full, 1)

            def gate_up(s, par, wait_chunk, ahead=1):
                pe.wait_ge(onehot_ok, s + ahead)
                for bank in range(2):
                    for half in range(2):
                        pe.matmul(ps[CAP * half:CAP * (half + 1), bank, :], onehot[par][:],
                                  bgu_sb[:, bank * D + half * HALF:bank * D + (half + 1) * HALF], start=True, stop=False,
                                  skip_group_check=True)
                pe.wait_ge(xT_ok, s + ahead)
                for k in range(KC):
                    w = wait_chunk(k)
                    lhsT = xT[par][:, (k % 4) * P + CAP * (k // 4):(k % 4) * P + CAP * (k // 4 + 1)]
                    for bank in range(2):
                        for half in range(2):
                            mm = pe.matmul(ps[CAP * half:CAP * (half + 1), bank, :], lhsT,
                                           w[:, bank * D + half * HALF:bank * D + (half + 1) * HALF], start=False,
                                           stop=(k == KC - 1), skip_group_check=True)
                    mm.then_inc(chunks_used, 1)

            def turn_gates(s, par, ahead=1):
                pe.wait_ge(selg_ok, s + ahead)
                for t in range(TC):
                    mm = pe.transpose(ps[:, bank_t[1], t * P:(t + 1) * P],
                                      selg[par][:, t, :, :].rearrange("p d s -> p (d s)"), ident[:])
                mm.then_inc(gT_full, 1)

            def turn_act(s):
                pe.wait_ge(act_ok, s + 1)
                pe.wait_ge(g_ok, s + 1)
                for j in range(4):
                    mm = pe.transpose(ps[:, bank_t[1], j * P:(j + 1) * P], act[:, j * P:(j + 1) * P], ident[:])
                mm.then_inc(aT_full, 1)

            def bias_down(par):
                for half in range(2):
                    pe.matmul(ps[CAP * half:CAP * (half + 1), bank_y, :], onehot[par][:],
                              bdn_sb[:, half * HALF:(half + 1) * HALF], start=True, stop=False, skip_group_check=True)

            def down(s, wait_chunk):
                pe.wait_ge(aT_ok, s + 1)
                for c in range(8, PER_EXPERT):
                    w = wait_chunk(c)
                    for a in range(2):
                        k = 2 * (c - 8) + a
                        lhsT = actT[:, (k % 4) * P + CAP * (k // 4):(k % 4) * P + CAP * (k // 4 + 1)]
                        for half in range(2):
                            mm = pe.matmul(ps[CAP * half:CAP * (half + 1), bank_y, :], lhsT,
                                           w[:, a * D + half * HALF:a * D + (half + 1) * HALF], start=False,
                                           stop=(k == KC - 1), skip_group_check=True)
                    mm.then_inc(chunks_used, 1)

            def scatter(s):
                pe.wait_ge(y_ok, s + 1)
                for t in range(TC):
                    for half in range(2):
                        rws = slice(CAP * half, CAP * (half + 1))
                        mm = pe.matmul(ps[:, (4 if t == 0 else 2) + half, :], g_sb[rws, t * P:(t + 1) * P],
                                       y_sb[rws, :], start=True, stop=True, skip_group_check=True)
                    mm.then_inc(sc_full, 1)

            keep_clock(3)
            pe.wait_ge(scaled, 2 + TC)
            gather(0)
            keep_clock(4)
            turn_tokens(0)
            pe.wait_ge(bgu_in, 16)
            pe.wait_ge(bdn_in, 16)
            most = load_most(pe)
            def experts(turn=None):
                e0 = 0 if turn is None else turn * UNROLL
                for u in range(UNROLL):
                    def ring_chunk(c, u=u):
                        return expert_chunk(pe, u * PER_EXPERT + c, turn)
                    s = e0 + u
                    gate_up(s, u % 2, ring_chunk)
                    gather(s + 1)
                    turn_gates(s, u % 2)
                    bias_down(u % 2)
                    turn_act(s)
                    turn_tokens(s + 1)
                    down(s, ring_chunk)
                    scatter(s)
            experts()
            with pe.Fori(1, E // UNROLL) as turn:
                experts(turn)

            def again(b, e, k):
                s = k + E
                def ring_chunk(c):
                    slot = SLOT_ORDER[c]
                    pe.wait_ge(slot_full[slot], k * 16 + 16 * (front_uses[slot] + len(range(c, total - EXTRA, RING)) + 1))
                    return ring[:, slot, :]
                gather(s + 1)
                turn_tokens(s + 1)
                gate_up(s, 0, ring_chunk, ahead=2)
                turn_gates(s, 0, ahead=2)
                bias_down(0)
                turn_act(s)
                down(s, ring_chunk)
                scatter(s)

            more_rounds(pe, most, again)

        @block.scalar
        def _(act_e):
            def copy(dst, src, done):
                act_e.activation(dst, src, ACT.Copy).then_inc(done, 1)

            def fetch_table(fn):
                fetched[0] += 1
                act_e.activation(warm[:], ones[:, 0:1], fn).then_inc(warmed, 1)
                act_e.wait_ge(warmed, fetched[0])
            fetched = [0]

            def square(n, c, src, junk, done):
                act_e.activation(junk[:, c, :], src[:, c, :], ACT.Square, scale=D ** -0.5,
                                 accum_out=stat[:, n - 1, 0, c:c + 1]).then_inc(done, 1)

            def root_of(n):
                act_e.wait_ge(squares, TC * n)
                act_e.activation(stat[:, n - 1, 1, :], stat[:, n - 1, 0, :], ACT.Sqrt, bias=eps[:]).then_inc(root, 1)

            def t_out(name, fn):
                b, n = t_use(name)
                act_e.wait_ge(t_full[b], n)
                fn(ps[:, bank_t[b], :], t_free[b])

            def with_gain(dst, row, pair):
                def fn(bank, done):
                    for c in range(2):
                        k = 2 * pair + c
                        ins = act_e.activation(dst[:, k, :], bank[:, c * SEQ:(c + 1) * SEQ], ACT.Copy,
                                               scale=vec[:, row + k:row + k + 1])
                    ins.then_inc(done, 1)
                return fn

            def a_out(name, dst):
                bank, done = a_complete(act_e, name)
                copy(dst, bank.rearrange("p (a b) -> p a b", a=2), done)

            def hi(*halves):
                for j in halves:
                    if j % 2 == 0:
                        act_e.wait_ge(slot_full[j // 2 % FRONT_RING], 16 * (j // 2 // FRONT_RING + 1))
                    if j >= HI_BUFS:
                        act_e.wait_ge(halves_used, j - HI_BUFS + 1)
                    src = half_of(j // 2, j % 2)
                    copy(w_hi[j % HI_BUFS][:].rearrange("p (k n) -> p k n", k=src.shape[1]), src, w_hi_ok)

            def hi_tiles(name, pair, dst, row):
                t_out(f"{name}{pair}", lambda bank, done: with_gain(dst, row, pair)(bank, hi_ok))

            act_e.wait_ge(consts, N_CONSTS)
            fetch_table(ACT.Sqrt)
            t_out("vec", lambda bank, done: copy(vec[:], bank[:, 0:N_ROWS], done))
            act_e.wait_ge(t_free[1], 1)
            hi_tiles("mem", 0, mn_hi, ROW_MEM), hi_tiles("mem", 1, mn_hi, ROW_MEM)
            hi(0)
            hi_tiles("mem", 2, mn_hi, ROW_MEM), hi_tiles("mem", 3, mn_hi, ROW_MEM)
            hi(1, 2, 3)
            for c in range(TC):
                act_e.wait_ge(x_in[c], 16)
                square(1, c, h_rows, x_squares, squares)
            root_of(1)
            hi(4, 5)
            for c in range(TC):
                act_e.wait_ge(mem_in[c], 16)
                square(2, c, mem_rows, mem_squares, squares)
            root_of(2)
            hi(6, 7, 8)
            hi_tiles("x", 0, hn_hi, ROW_MIX), hi_tiles("x", 1, hn_hi, ROW_MIX)
            hi(9, 10)
            hi_tiles("x", 2, hn_hi, ROW_MIX), hi_tiles("x", 3, hn_hi, ROW_MIX)
            hi(11)
            act_e.wait_ge(mem_rstd_ok, 1)
            for r in range(4):
                row_complete(act_e, "w_v", r)
                act_e.activation(v_rows[:, r % 2, (r // 2) * HALF:(r // 2 + 1) * HALF], ps[:, bank_row[r], :], ACT.Copy,
                                 scale=stat[:, 1, 2, r % 2:r % 2 + 1]).then_inc(row_free, 1)
            hi(12)
            a_out("u0", u_pad[:, 0:2, PAD:])
            hi(13, 14)
            a_out("u1", u_pad[:, 2:4, PAD:])
            hi(15, 16)
            a_out("C0", c_buf[:])
            hi(17, 18, 19, 20, 21, 22)
            act_e.wait_ge(z_used, 1)
            a_out("C1", c_buf[:])
            hi(*range(23, 39))
            act_e.wait_ge(h_added, 4)
            for c in range(TC):
                square(3, c, h_rows, x_squares, squares)
            root_of(3)
            hi(39, 40, 41)
            hi_tiles("h", 0, hn_hi, ROW_XATTN), hi_tiles("h", 1, hn_hi, ROW_XATTN)
            hi(42)
            hi_tiles("h", 2, hn_hi, ROW_XATTN), hi_tiles("h", 3, hn_hi, ROW_XATTN)
            hi(43)

            def softmax(h):
                n = a_use(f"s{h}")
                act_e.wait_ge(neg_max, h + 1)
                for t in range(TC):
                    ins = act_e.activation(probs[:, t, h, :], ps[:, n % 2, t * SEQ:(t + 1) * SEQ], ACT.Exp,
                                           bias=smax[:, 1, h, t:t + 1], scale=HEAD_DIM ** -0.5,
                                           accum_out=smax[:, 2, h, t:t + 1])
                    ins.then_inc(exps, 1)
                act_e.wait_ge(exps, TC * (h + 1))
                act_e.sem_inc(a_free[n % 2], 1)

            def out_head(h):
                bank, _ = a_complete(act_e, f"o{h}")
                copy(hn_hi[:, 2 * h:2 * h + 2, :], bank.rearrange("p (a b) -> p a b", a=2), hi_ok)

            def turned(h):
                t_out(f"P{h}", lambda bank, done: copy(probsT[:, h, :, :], bank.rearrange("p (c t) -> p c t", c=TC), done))

            def query(h):
                a_out(f"q{h}", qT[:, 2 * h:2 * h + 2, :])
            hi(44), query(0), hi(45, 46), query(1), hi(47), softmax(0)
            hi(48), query(2), hi(49), softmax(1)
            hi(50), query(3), hi(51), softmax(2), turned(1), softmax(3)
            out_head(0), out_head(1), turned(3)
            hi(52, 53), out_head(2)
            hi(54, 55), out_head(3)
            fetch_table(ACT.Sqrt)
            act_e.wait_ge(h_added, 8)
            for c in range(TC):
                square(4, c, h_rows, x_squares, squares)
            root_of(4)
            fetch_table(ACT.Exp)
            act_e.wait_ge(rstd_ok, 1)
            for c in range(TC):
                act_e.activation(n_rows[:, c, :], h_rows[:, c, :], ACT.Copy, scale=stat[:, 3, 2, c:c + 1]).then_inc(scaled, 1)
            act_e.wait_ge(route_neg, 1)
            for t in range(TC):
                act_e.activation(ex[:, t, :], lg[:, t, 0:E], ACT.Exp, bias=small[:, 0, t:t + 1]).then_inc(route_exp, 1)

            def tokens_out(s):
                act_e.wait_ge(xg_full, s + 1)
                copy(xg_sb[:], ps[:, bank_xg, :], xg_ok)

            def sigmoid(s):
                act_e.wait_ge(glu_ok, s + 1)
                act_e.activation(sig[:], glu[:], ACT.Sigmoid, scale=ALPHA).then_inc(sig_ok, 1)

            def gates_out(s):
                act_e.wait_ge(gT_full, s + 1)
                copy(g_sb[:], ps[:, bank_t[1], 0:SEQ], g_ok)

            def act_out(s):
                act_e.wait_ge(aT_full, s + 1)
                copy(actT[:], ps[:, bank_t[1], :], aT_ok)

            def y_out(s):
                act_e.wait_ge(chunks_used, s * PER_EXPERT + PER_EXPERT)
                copy(y_sb[:], ps[:, bank_y, :], y_ok)

            fetch_table(ACT.Sigmoid)
            tokens_out(0)
            most = load_most(act_e)
            with act_e.Fori(0, E) as s:
                sigmoid(s)
                tokens_out(s + 1)
                gates_out(s)
                act_out(s)
                y_out(s)

            def again(b, e, k):
                s = k + E
                tokens_out(s + 1)
                sigmoid(s)
                gates_out(s)
                act_out(s)
                y_out(s)
            k = more_rounds(act_e, most, again)
            fetch_table(ACT.Sqrt)
            for c in range(TC):
                act_e.wait_ge(sc_added, k * TC + (E * TC - TC + c + 1))
                square(5, c, h_rows, h_squares, end_squares)
                act_e.wait_ge(end_squares, c + 1)
                act_e.activation(stat[:, 4, 1, c:c + 1], stat[:, 4, 0, c:c + 1], ACT.Sqrt, bias=eps[:]).then_inc(end_root, 1)

        @block.vector
        def _(dve):
            links = [0]

            def linked(ins):
                links[0] += 1
                ins.then_inc(link, 1)
                dve.wait_ge(link, links[0])

            def newton(ln, n, c=None):
                t = slice(0, TC) if c is None else slice(c, c + 1)
                square, root_n, rstd, scratch = (stat[:, n - 1, i, t] for i in range(4))
                ln(dve.reciprocal(rstd, root_n))
                ln(dve.scalar_tensor_tensor(out=scratch, in0=rstd, scalar=-0.5, in1=rstd, op0=ALU.mult, op1=ALU.mult))
                ln(dve.scalar_tensor_tensor(out=scratch, in0=square, scalar=EPS, in1=scratch, op0=ALU.add, op1=ALU.mult))
                ln(dve.scalar_tensor_tensor(out=rstd, in0=scratch, scalar=1.5, in1=rstd, op0=ALU.add, op1=ALU.mult))

            def find_rstd(n):
                dve.wait_ge(squares, TC * n)
                dve.wait_ge(root, n)
                newton(linked, n)

            def normalise(n, times):
                linked(dve.tensor_scalar(n_rows[:, 0, :], h_rows[:, 0, :], stat[:, n - 1, 2, 0:1], None, ALU.mult))
                dve.tensor_scalar(n_rows[:, 1, :], h_rows[:, 1, :], stat[:, n - 1, 2, 1:2], None, ALU.mult).then_inc(scaled, 1)
                dve.wait_ge(scaled, times)

            def t_with_gain(name, dst, row, pair):
                b, n = t_use(f"{name}{pair}")
                dve.wait_ge(t_full[b], n)
                gain = vec[:, row + 2 * pair:row + 2 * pair + 2].unsqueeze(2).broadcast_to([P, 2, SEQ])
                dve.tensor_tensor(dst[:, 2 * pair:2 * pair + 2, :],
                                  ps[:, bank_t[b], :].rearrange("p (c t) -> p c t", c=2), gain,
                                  ALU.mult).then_inc(t_free[b], 1)

            def lo_tiles(name, pair, dst_hi, dst, row):
                b, _ = t_use(f"{name}{pair}")
                dve.wait_ge(hi_ok, HI_ORDER.index(f"{name}{pair}") + 1)
                for c in range(2):
                    k = 2 * pair + c
                    ins = dve.scalar_tensor_tensor(out=dst[:, k, :], in0=ps[:, bank_t[b], c * SEQ:(c + 1) * SEQ],
                                                   scalar=vec[:, row + k:row + k + 1],
                                                   in1=dst_hi[:, k, :].bitcast(F32), op0=ALU.mult, op1=ALU.subtract)
                ins.then_inc(t_free[b], 1)

            for pair in range(4):
                lo_tiles("mem", pair, mn_hi, mn_lo, ROW_MEM)
            for c in range(TC):
                dve.wait_ge(x_in[c], 16)
            find_rstd(1)
            normalise(1, 1)
            find_rstd(2)
            dve.sem_inc(mem_rstd_ok, 1)
            dve.wait_ge(consts, N_CONSTS)
            linked(dve.tensor_scalar(z_acc[:, 0:P], ident[:], stat[:, 1, 2, 0:1], None, ALU.mult))
            dve.tensor_scalar(z_acc[:, P:2 * P], ident[:], stat[:, 1, 2, 1:2], None, ALU.mult).then_inc(diag_ok, 1)
            linked(dve.reciprocal(count_r[:], count_r[:]))
            for pair in range(4):
                lo_tiles("x", pair, hn_hi, hn_lo, ROW_MIX)
            for g, w in enumerate(WINDOWS):
                if g == 2:
                    b, n = t_use("scale")
                    dve.wait_ge(t_full[b], n)
                    dve.tensor_copy(mem_scale[:], ps[:, bank_t[b], 0:SEQ]).then_inc(t_free[b], 1)
                    dve.wait_ge(t_free[b], n)
                if g % 2 == 0:
                    n = a_use(f"u{g // 2}")
                    dve.wait_ge(a_free[n % 2], n // 2 + 1)
                src, span, buf = u_pad[:, g, :], 1, 0
                while span < w:
                    lo = 2 * span - 1
                    linked(dve.tensor_tensor(win[buf][:, lo:], src[:, lo:], src[:, lo - span:PAD + SEQ - span], ALU.add))
                    src, span, buf = win[buf], 2 * span, 1 - buf
                frame = u_pad[:, g, :]
                linked(dve.tensor_tensor(early[:, 0:w], src[:, PAD:PAD + w], count_r[:, 0:w], ALU.mult))
                linked(dve.tensor_tensor(frame[:, PAD:PAD + w], early[:, 0:w], frame[:, PAD:PAD + w], ALU.subtract))
                dve.scalar_tensor_tensor(out=frame[:, PAD + w:], in0=src[:, PAD + w:], scalar=1.0 / w,
                                         in1=frame[:, PAD + w:], op0=ALU.mult, op1=ALU.subtract).then_inc(pooled, 1)
                dve.wait_ge(pooled, g + 1)
            def conv_in(i):
                n = a_use(f"C{i}")
                dve.wait_ge(a_free[n % 2], n // 2 + 1)
                bank, done = a_complete(dve, f"v{i}")
                dve.tensor_tensor(z_pad[:, :, 2:], bank.rearrange("p (a t) -> p a t", a=2), c_buf[:],
                                  ALU.mult).then_inc(done, 1)
                dve.wait_ge(done, a_use(f"v{i}") // 2 + 1)
                dve.sem_inc(z_used, 1)

            tiles = [0]

            def mix_done(ins):
                tiles[0] += 1
                ins.then_inc(mixed, 1)
                dve.wait_ge(mixed, tiles[0])

            def conv_out(i):
                bank, done = a_complete(dve, f"B{i}")
                for a in range(2):
                    def tap(k):
                        r = ROW_CONV + GROUPS * k + 2 * i + a
                        return vec[:, r:r + 1]
                    linked(dve.tensor_scalar(z_acc[:], z_pad[:, a, 2:], tap(2), None, ALU.mult))
                    for k in (1, 0):
                        linked(dve.scalar_tensor_tensor(out=z_acc[:], in0=z_pad[:, a, k:k + SEQ], scalar=tap(k),
                                                        in1=z_acc[:], op0=ALU.mult, op1=ALU.add))
                    linked(dve.tensor_tensor(z_acc[:], bank[:, a * SEQ:(a + 1) * SEQ], z_acc[:], ALU.mult))
                    linked(dve.tensor_copy(mix_hi[:, 4 + 2 * i + a, :], z_acc[:]))
                    mix_done(dve.tensor_tensor(mix_lo[:, 4 + 2 * i + a, :], z_acc[:],
                                               mix_hi[:, 4 + 2 * i + a, :].bitcast(F32), ALU.subtract))
                dve.sem_inc(done, 1)

            def pool_out(i):
                bank, done = a_complete(dve, f"pool{i}")
                for a in range(2):
                    g = 2 * i + a
                    scale = vec[:, ROW_POOL + g:ROW_POOL + g + 1]
                    linked(dve.tensor_scalar(mix_hi[:, g, :], bank[:, a * SEQ:(a + 1) * SEQ], scale, None, ALU.mult))
                    mix_done(dve.scalar_tensor_tensor(out=mix_lo[:, g, :], in0=bank[:, a * SEQ:(a + 1) * SEQ],
                                                      scalar=scale, in1=mix_hi[:, g, :].bitcast(F32), op0=ALU.mult,
                                                      op1=ALU.subtract))
                dve.sem_inc(done, 1)

            def keys_out(c):
                bank, done = a_complete(dve, f"k{c}")
                dve.tensor_tensor(kT[:, 2 * c:2 * c + 2, :], bank.rearrange("p (a m) -> p a m", a=2),
                                  mem_scale[:].unsqueeze(1).broadcast_to([P, 2, SEQ]), ALU.mult).then_inc(done, 1)
            conv_in(0), conv_out(0)
            pool_out(0), conv_in(1), pool_out(1), conv_out(1)
            keys_out(0)

            def add_rows(use):
                for r in range(4):
                    row_complete(dve, use, r)
                    part = h_rows[:, r % 2, (r // 2) * HALF:(r // 2 + 1) * HALF]
                    dve.tensor_tensor(part, ps[:, bank_row[r], :], part, ALU.add).then_inc(h_added, 1)
            add_rows("w_out")
            dve.wait_ge(h_added, 4)
            find_rstd(3)
            normalise(3, 2)
            keys_out(1)
            lo_tiles("h", 0, hn_hi, hn_lo, ROW_XATTN), lo_tiles("h", 1, hn_hi, hn_lo, ROW_XATTN)
            keys_out(2)
            lo_tiles("h", 2, hn_hi, hn_lo, ROW_XATTN), lo_tiles("h", 3, hn_hi, hn_lo, ROW_XATTN)
            keys_out(3)

            def largest(h):
                bank, _ = a_complete(dve, f"s{h}")
                linked(dve.tensor_reduce(smax[:, 0, h, :], bank.rearrange("p (c m) -> p c m", c=TC), AX.X, ALU.max))
                dve.tensor_scalar(smax[:, 1, h, :], smax[:, 0, h, :], -HEAD_DIM ** -0.5, None, ALU.mult).then_inc(neg_max, 1)

            def scale_probs(h):
                dve.wait_ge(exps, TC * (h + 1))
                linked(dve.reciprocal(smax[:, 3, h, :], smax[:, 2, h, :]))
                linked(dve.tensor_scalar(probs[:, 0, h, :], probs[:, 0, h, :], smax[:, 3, h, 0:1], None, ALU.mult))
                dve.tensor_scalar(probs[:, 1, h, :], probs[:, 1, h, :], smax[:, 3, h, 1:2], None, ALU.mult).then_inc(probs_ok, 1)

            def turned(h):
                b, n = t_use(f"P{h}")
                dve.wait_ge(t_full[b], n)
                dve.tensor_copy(probsT[:, h, :, :], ps[:, bank_t[b], :].rearrange("p (c t) -> p c t", c=TC)).then_inc(t_free[b], 1)

            def out_head(h):
                bank, done = a_complete(dve, f"o{h}")
                dve.wait_ge(hi_ok, HI_ORDER.index(f"o{h}") + 1)
                dve.tensor_tensor(hn_lo[:, 2 * h:2 * h + 2, :], bank.rearrange("p (a b) -> p a b", a=2),
                                  hn_hi[:, 2 * h:2 * h + 2, :].bitcast(F32), ALU.subtract).then_inc(done, 1)
            largest(0), scale_probs(0), largest(1), turned(0), scale_probs(1)
            largest(2), largest(3), scale_probs(2), scale_probs(3)
            out_head(0), turned(2), out_head(1), out_head(2), out_head(3)
            add_rows("w_o")
            for pair in range(4):
                t_with_gain("g", gT, ROW_MOE, pair)
            find_rstd(4)
            dve.sem_inc(rstd_ok, 1)

            def linked_pair(step):
                for t in range(TC):
                    step(t).then_inc(link, 1)
                links[0] += TC
                dve.wait_ge(link, links[0])
            a_complete(dve, "logits")
            dve.wait_ge(consts, N_CONSTS)
            dve.wait_ge(br_in, 16)
            linked_pair(lambda t: dve.scalar_tensor_tensor(out=lg[:, t, 0:E], in0=ps[:, t, 0:E], scalar=stat[:, 3, 2, t:t + 1],
                                                           in1=br_sb[:], op0=ALU.mult, op1=ALU.add))
            linked_pair(lambda t: dve.max(top[:, t, :], lg[:, t, 0:E]))
            linked(dve.memset(top[:, :, TOP_K:8], -FAR))
            linked_pair(lambda t: dve.match_replace(marked[:, t, :], top[:, t, :], lg[:, t, :], FAR))
            for t in range(TC):
                dve.tensor_scalar(mask[:, t, :], marked[:, t, 0:E], FAR, None, ALU.is_equal).then_inc(masked, 1)
            dve.tensor_scalar(small[:, 0, :], top[:, :, 0], -1.0, None, ALU.mult).then_inc(route_neg, 1)
            dve.wait_ge(masked, TC)

            def gates():
                dve.wait_ge(route_exp, TC)
                linked_pair(lambda t: dve.scalar_tensor_tensor(out=gate[:, t, 0:E], in0=ex[:, t, :], scalar=1.0,
                                                               in1=mask[:, t, :], op0=ALU.mult, op1=ALU.mult,
                                                               accum_out=small[:, 1, t:t + 1]))
                linked(dve.reciprocal(small[:, 2, :], small[:, 1, :]))
                linked_pair(lambda t: dve.tensor_scalar(gate[:, t, 0:E], gate[:, t, 0:E], small[:, 2, t:t + 1], None,
                                                        ALU.mult))

            def places():
                dve.wait_ge(ranked, 1)
                ranks = ps[:, 0, 0:TC * E].rearrange("p (c e) -> p c e", c=TC)
                linked(dve.scalar_tensor_tensor(out=place[:, :, 0:E], in0=ranks, scalar=1.0, in1=mask[:],
                                                op0=ALU.add, op1=ALU.mult))

            def counts():
                dve.wait_ge(counted, 1)
                number = ps[0:1, 1, 0:E]
                linked(dve.tensor_copy(cnt_i[:], number))
                linked(dve.tensor_reduce(most_f[:], number, AX.X, ALU.max))
                dve.tensor_copy(most_i[:], most_f[:]).then_inc(routed, 1)

            def select(s, e, par, shift=0):
                at = place[:, :, bass.ds(e, 1)].broadcast_to([P, TC, CAP])
                slots = slot_no[:].unsqueeze(1).broadcast_to([P, TC, CAP])
                if shift:
                    dve.scalar_tensor_tensor(out=sel[:], in0=at, scalar=float(shift), in1=slots, op0=ALU.subtract,
                                             op1=ALU.is_equal).then_inc(sel_ok, 1)
                else:
                    dve.tensor_tensor(sel[:], slots, at, ALU.is_equal).then_inc(sel_ok, 1)
                dve.tensor_copy(onehot[par][:], ident[0:E, bass.ds(e, 1)].broadcast_to([E, CAP])).then_inc(onehot_ok, 1)

            def weigh(s, e, par):
                dve.wait_ge(sel_ok, s + 1)
                for d in range(2):
                    ins = dve.tensor_tensor(selg[par][:, :, d, :], sel[:],
                                            gate[:, :, bass.ds(e, 1)].broadcast_to([P, TC, CAP]), ALU.mult)
                ins.then_inc(selg_ok, 1)
                dve.wait_ge(selg_ok, s + 1)

            def tokens_out(s, par):
                dve.wait_ge(xT_full, s + 1)
                gain = vec[:, ROW_MOE:ROW_MOE + KC].rearrange("p (h j) -> p j h", h=2).unsqueeze(3).broadcast_to([P, 4, 2, CAP])
                dve.tensor_tensor(xT[par][:].rearrange("p (j h s) -> p j h s", j=4, h=2),
                                  ps[:, bank_t[0], :].rearrange("p (j h s) -> p j h s", j=4, h=2), gain,
                                  ALU.mult).then_inc(xT_ok, 1)

            def activate(s):
                dve.wait_ge(chunks_used, s * PER_EXPERT + KC)
                dve.tensor_scalar(glu[:], ps[:, 0, :], LIMIT, None, ALU.min).then_inc(glu_ok, 1)
                dve.tensor_scalar(lin[:], ps[:, 1, :], LIMIT, -LIMIT, ALU.min, ALU.max).then_inc(step_link, 1)
                dve.wait_ge(glu_ok, s + 1)
                dve.wait_ge(step_link, s * 2 + 1)
                dve.scalar_tensor_tensor(out=lin[:], in0=lin[:], scalar=1.0, in1=glu[:], op0=ALU.add, op1=ALU.mult).then_inc(step_link, 1)
                dve.wait_ge(step_link, s * 2 + 2)
                dve.wait_ge(sig_ok, s + 1)
                dve.tensor_tensor(act[:], lin[:], sig[:], ALU.mult).then_inc(act_ok, 1)

            def add_back(s):
                for t in range(TC):
                    b = 4 if t == 0 else 2
                    dve.wait_ge(sc_full, s * TC + t + 1)
                    dve.tensor_tensor(h_rows[:, t, :].rearrange("p (a n) -> p a n", a=2), ps[:, b:b + 2, :],
                                      h_rows[:, t, :].rearrange("p (a n) -> p a n", a=2), ALU.add).then_inc(sc_added, 1)
                dve.wait_ge(sc_added, s * TC + TC)

            places()
            select(0, 0, 0)
            gates()
            counts()
            weigh(0, 0, 0)
            tokens_out(0, 0)
            most = load_most(dve)
            with dve.Fori(0, E // UNROLL) as turn:
                e0 = turn * UNROLL
                for u in range(UNROLL):
                    s = e0 + u
                    select(s + 1, s + 1, (u + 1) % 2)
                    weigh(s + 1, s + 1, (u + 1) % 2)
                    activate(s)
                    tokens_out(s + 1, (u + 1) % 2)
                    add_back(s)

            def again(b, e, k):
                s = k + E
                select(s + 1, e, 0, shift=CAP * b)
                weigh(s + 1, e, 0)
                tokens_out(s + 1, 0)
                activate(s)
                add_back(s)
            k = more_rounds(dve, most, again)
            ends = [0]

            def end_linked(ins):
                ends[0] += 1
                ins.then_inc(end_link, 1)
                dve.wait_ge(end_link, ends[0])
            dve.wait_ge(gfin_in, 16)
            dve.wait_ge(sc_added, k * TC + E * TC)
            for c in range(TC):
                dve.wait_ge(end_squares, c + 1)
                dve.wait_ge(end_root, c + 1)
                newton(end_linked, 5, c)
                for half in range(2):
                    part = slice(half * HALF, (half + 1) * HALF)
                    dve.scalar_tensor_tensor(out=n_rows[:, c, part], in0=h_rows[:, c, part],
                                             scalar=stat[:, 4, 2, c:c + 1], in1=gfin[:, part], op0=ALU.mult,
                                             op1=ALU.mult).then_inc(end_out, 1)


_INS = ["x", "mem", "g_mix", "w_in", "w_pool", "pool_scale", "conv_w", "w_out", "g_xattn", "g_mem", "w_q", "w_k", "w_v",
        "w_o", "g_moe", "w_router", "b_router", "w_gate_up", "b_gate_up", "w_down", "b_down", "g_final"]


def kernel(**inputs):
    import concourse.bacc as bacc
    from concourse.bass_utils import run_bass_kernel_spmd

    nc = bacc.Bacc("TRN2", target_bir_lowering=False, num_devices=1)
    arrays, args = {}, []
    for name in _INS:
        a = np.ascontiguousarray(inputs[name])
        arrays[f"in_{name}"] = a
        args.append(nc.dram_tensor(f"in_{name}", a.shape, mybir.dt.from_np(a.dtype), kind="ExternalInput").ap())
    out = nc.dram_tensor("out_h", (1, SEQ, D), F32, kind="ExternalOutput").ap()
    program(nc, *args, out)
    r = run_bass_kernel_spmd(nc, [arrays], core_ids=[0])
    return r.results[0]["out_h"]
```
